# Optimizing a Trainium2 kernel written in Bass

```python
import jax, jax.numpy as jnp
from jax import lax
import numpy as np
import math

D_MODEL = 1024
BATCH = 1
SEQ = 512
DEPTH = 2

D_CONV = D_MODEL
CONV_WIDTH = 3
RET_HEADS = 4
RET_QK_DIM = 128
RET_V_DIM = 256
RET_QK = RET_HEADS * RET_QK_DIM
RET_V = RET_HEADS * RET_V_DIM
CHUNK = 128
ROPE_BASE = 10000.0
D_FF = 4 * D_MODEL
EPS = 1e-6
MAX_START = 1024

IN_SIZES = (D_CONV, D_CONV, D_CONV, RET_QK, RET_QK, RET_V, RET_V, D_MODEL, D_MODEL)
D_IN = 3 * D_CONV + 2 * RET_QK + 2 * RET_V + 2 * D_MODEL


def rmsnorm(x, g):
    xf = x.astype(jnp.float32)
    xf = xf * lax.rsqrt(jnp.mean(xf * xf, axis=-1, keepdims=True) + EPS)
    return (xf * g.astype(jnp.float32)).astype(x.dtype)

def rotary(t, positions):
    half = t.shape[-1] // 2
    inv_freq = ROPE_BASE ** (-jnp.arange(half, dtype=jnp.float32) / half)
    ang = positions.astype(jnp.float32)[..., None] * inv_freq
    cos = jnp.cos(ang)[:, :, None, :].astype(t.dtype)
    sin = jnp.sin(ang)[:, :, None, :].astype(t.dtype)
    t1, t2 = t[..., :half], t[..., half:]
    return jnp.concatenate([t1 * cos - t2 * sin, t1 * sin + t2 * cos], axis=-1)

def short_conv_mixer(b, c, u, conv_w, w_out):
    z = c * u
    z = lax.conv_general_dilated(
        z, conv_w[:, None, :].astype(z.dtype), window_strides=(1,),
        padding=[(CONV_WIDTH - 1, 0)], dimension_numbers=("NWC", "WIO", "NWC"),
        feature_group_count=D_CONV)
    return (b * z) @ w_out

def retention_core(q, k, v, positions):
    bsz, seq = q.shape[0], q.shape[1]
    n_chunks = seq // CHUNK
    q = rotary(q, positions) * (RET_QK_DIM ** -0.5)
    k = rotary(k, positions)

    def to_chunks(t):
        return t.astype(jnp.float32).reshape(bsz, n_chunks, CHUNK, RET_HEADS, t.shape[-1]).swapaxes(0, 1)

    qc, kc, vc = to_chunks(q), to_chunks(k), to_chunks(v)
    log_gamma = jnp.log1p(-jnp.exp2(-5.0 - jnp.arange(RET_HEADS, dtype=jnp.float32)))
    pos = jnp.arange(CHUNK, dtype=jnp.float32)
    rel = pos[:, None] - pos[None, :]
    decay_intra = jnp.where(rel >= 0, jnp.exp(log_gamma[:, None, None] * jnp.maximum(rel, 0.0)), 0.0)
    decay_q = jnp.exp((pos[:, None] + 1.0) * log_gamma)
    decay_k = jnp.exp((CHUNK - 1.0 - pos[:, None]) * log_gamma)
    decay_chunk = jnp.exp(CHUNK * log_gamma)

    scores = jnp.einsum("nbqhd,nbkhd->nbhqk", qc, kc) * decay_intra
    o_intra = jnp.einsum("nbhqk,nbkhv->nbqhv", scores, vc)

    def step(state, inp):
        q_i, k_i, v_i = inp
        o_inter = jnp.einsum("bqhd,bhdv->bqhv", q_i, state) * decay_q[None, :, :, None]
        state = state * decay_chunk[None, :, None, None] + jnp.einsum("bkhd,kh,bkhv->bhdv", k_i, decay_k, v_i)
        return state, o_inter

    state0 = jnp.zeros((bsz, RET_HEADS, RET_QK_DIM, RET_V_DIM), jnp.float32)
    _, o_inter = lax.scan(step, state0, (qc, kc, vc))
    return (o_intra + o_inter).swapaxes(0, 1).reshape(bsz, seq, RET_HEADS, RET_V_DIM)

def retention_mixer(q, k, v, g, positions, ret_norm, w_out):
    bsz, seq = q.shape[0], q.shape[1]
    o = retention_core(q.reshape(bsz, seq, RET_HEADS, RET_QK_DIM),
                       k.reshape(bsz, seq, RET_HEADS, RET_QK_DIM),
                       v.reshape(bsz, seq, RET_HEADS, RET_V_DIM), positions)
    mu = jnp.mean(o, axis=-1, keepdims=True)
    var = jnp.mean(jnp.square(o - mu), axis=-1, keepdims=True)
    o = ((o - mu) * lax.rsqrt(var + EPS)).reshape(bsz, seq, RET_V) * ret_norm.astype(jnp.float32)
    o = o.astype(g.dtype)
    return (jax.nn.silu(g) * o) @ w_out

def hybrid_layer(x, positions, norm_mix, w_in, conv_w, w_conv_out, ret_norm, w_ret_out, w_o,
                 norm_mlp, w_up, w_down):
    h = rmsnorm(x, norm_mix)
    proj = h @ w_in
    split_points = np.cumsum(IN_SIZES)[:-1].tolist()
    cb, cc, cu, q, k, v, g, ga, gb = jnp.split(proj, split_points, axis=-1)
    y_conv = short_conv_mixer(cb, cc, cu, conv_w, w_conv_out)
    y_ret = retention_mixer(q, k, v, g, positions, ret_norm, w_ret_out)
    merged = jax.nn.sigmoid(ga) * y_conv + jax.nn.sigmoid(gb) * y_ret
    x = x + merged @ w_o
    h2 = rmsnorm(x, norm_mlp)
    return x + jnp.square(jax.nn.relu(h2 @ w_up)) @ w_down

def first_inputs(seed: int = 0) -> dict:
    key = jax.random.key(seed)
    ks = jax.random.split(key, 14)
    f32 = jnp.float32

    def dense(k, fan_in, fan_out):
        return jax.random.normal(k, (DEPTH, fan_in, fan_out), f32) * (fan_in ** -0.5)

    def gain(k, shape):
        return 1.0 + 0.02 * jax.random.normal(k, shape, f32)

    x = jax.random.normal(ks[0], (BATCH, SEQ, D_MODEL), f32)
    start = jax.random.randint(ks[1], (BATCH, 1), 0, MAX_START, dtype=jnp.int32)
    positions = (start + jnp.arange(SEQ, dtype=jnp.int32)[None, :]).astype(jnp.int32)
    return {
        "x": x,
        "positions": positions,
        "norm_mix": gain(ks[2], (DEPTH, D_MODEL)),
        "w_in": dense(ks[3], D_MODEL, D_IN),
        "conv_w": jax.random.normal(ks[4], (DEPTH, CONV_WIDTH, D_CONV), f32) * (CONV_WIDTH ** -0.5),
        "w_conv_out": dense(ks[5], D_CONV, D_MODEL),
        "ret_norm": gain(ks[6], (DEPTH, RET_V)),
        "w_ret_out": dense(ks[7], RET_V, D_MODEL),
        "w_o": dense(ks[8], D_MODEL, D_MODEL),
        "norm_mlp": gain(ks[9], (DEPTH, D_MODEL)),
        "w_up": dense(ks[10], D_MODEL, D_FF),
        "w_down": dense(ks[11], D_FF, D_MODEL),
        "norm_final": gain(ks[12], (D_MODEL,)),
    }

def first_block(x, positions, norm_mix, w_in, conv_w, w_conv_out, ret_norm, w_ret_out, w_o,
              norm_mlp, w_up, w_down, norm_final):
    for i in range(DEPTH):
        x = hybrid_layer(x, positions, norm_mix[i], w_in[i], conv_w[i], w_conv_out[i], ret_norm[i],
                         w_ret_out[i], w_o[i], norm_mlp[i], w_up[i], w_down[i])
    return rmsnorm(x, norm_final)


DEPTH_2 = 1

GRID_W = 64
CTX_LEN = 256
N_MIXERS = 2
N_MOD = 6
NORM_EPS = 1e-6

NA_HEADS = 16
NA_HEAD_DIM = D_MODEL // NA_HEADS
NA_WIN_H = 8
NA_WIN_W = 16

HY_FILTER_WIDTH = 64
HY_EMB_DIM = 33
HY_BANDS = (HY_EMB_DIM - 1) // 2
HY_SHORT_WIDTH = 3
HY_DECAY_TARGET = 1e-2
HY_SHORT_DECAY_PCT = 0.3
HY_LONG_DECAY_PCT = 1.5

D_FF_2 = 2816
FFN_CONV_WIDTH = 3


def rms_norm(x, gain):
    xf = x.astype(jnp.float32)
    y = xf * lax.rsqrt(jnp.mean(xf * xf, axis=-1, keepdims=True) + NORM_EPS)
    return (y * gain.astype(jnp.float32)).astype(x.dtype)

def adaln(cond, w_mod, b_mod):
    return jnp.split(jax.nn.silu(cond) @ w_mod + b_mod, N_MOD, axis=-1)

def modulate(h, shift, scale):
    return h * (1.0 + scale) + shift

def dwconv_centred(x, w, b):
    k = w.shape[0]
    L = x.shape[1]
    pad = k // 2
    xp = jnp.pad(x, ((0, 0), (pad, k - 1 - pad), (0, 0)))
    out = xp[:, 0:L] * w[0]
    for i in range(1, k):
        out = out + xp[:, i:i + L] * w[i]
    return out + b

def split_heads(t):
    return t.reshape(t.shape[0], t.shape[1], NA_HEADS, NA_HEAD_DIM)

def neighbourhood_attention(q, k, v, k_ctx, v_ctx, rpb):
    B, L, H, Dh = q.shape
    rows = L // GRID_W
    kh = min(NA_WIN_H, rows)
    kw = NA_WIN_W
    scale = Dh ** -0.5
    cols = np.arange(GRID_W)
    col_idx = (np.clip(cols - kw // 2, 0, GRID_W - kw)[:, None] + np.arange(kw)[None, :]).astype(np.int32)
    dc_idx = (col_idx - cols[:, None] + (NA_WIN_W - 1)).astype(np.int32)
    qg = jnp.moveaxis(q.reshape(B, rows, GRID_W, H, Dh), 1, 0)
    kg = k.reshape(B, rows, GRID_W, H, Dh)
    vg = v.reshape(B, rows, GRID_W, H, Dh)

    def one_row(args):
        r, q_row = args
        r0 = jnp.clip(r - kh // 2, 0, rows - kh)
        k_win = lax.dynamic_slice_in_dim(kg, r0, kh, axis=1)[:, :, col_idx]
        v_win = lax.dynamic_slice_in_dim(vg, r0, kh, axis=1)[:, :, col_idx]
        dr_idx = r0 + jnp.arange(kh, dtype=jnp.int32) - r + (NA_WIN_H - 1)
        bias = rpb[:, dr_idx[:, None, None], dc_idx[None, :, :]]
        s_loc = jnp.einsum('bqhd,biqjhd->bhqij', q_row, k_win) * scale + jnp.transpose(bias, (0, 2, 1, 3))[None]
        s_ctx = jnp.einsum('bqhd,bkhd->bhqk', q_row, k_ctx) * scale
        s = jnp.concatenate([s_loc.reshape(B, H, GRID_W, kh * kw), s_ctx], axis=-1)
        p = jax.nn.softmax(s.astype(jnp.float32), axis=-1).astype(v.dtype)
        p_loc = p[..., :kh * kw].reshape(B, H, GRID_W, kh, kw)
        return (jnp.einsum('bhqij,biqjhd->bqhd', p_loc, v_win)
                + jnp.einsum('bhqk,bkhd->bqhd', p[..., kh * kw:], v_ctx))

    out = lax.map(one_row, (jnp.arange(rows, dtype=jnp.int32), qg))
    return jnp.moveaxis(out, 0, 1).reshape(B, L, H * Dh)

def context_attention(q, k, v):
    s = jnp.einsum('bqhd,bkhd->bhqk', q, k) * (q.shape[-1] ** -0.5)
    p = jax.nn.softmax(s.astype(jnp.float32), axis=-1).astype(v.dtype)
    o = jnp.einsum('bhqk,bkhd->bqhd', p, v)
    return o.reshape(o.shape[0], o.shape[1], -1)

def hyena_filters(L, w1, b1, w2, b2, w3, b3, w_out, sin_freq):
    f32 = jnp.float32
    t = jnp.linspace(0.0, 1.0, L, dtype=f32)[:, None]
    w = (2.0 * math.pi / L) * jnp.arange(L, dtype=f32)[:, None]
    bands = jnp.linspace(1e-4, HY_BANDS - 1, HY_BANDS, dtype=f32)[None, :]
    z = jnp.concatenate([t, jnp.cos(bands * w), -jnp.sin(bands * w)], axis=-1)
    freq = sin_freq.astype(f32)
    hdn = jnp.sin(freq * (z @ w1.astype(f32) + b1.astype(f32)))
    hdn = jnp.sin(freq * (hdn @ w2.astype(f32) + b2.astype(f32)))
    hdn = jnp.sin(freq * (hdn @ w3.astype(f32) + b3.astype(f32)))
    h = (hdn @ w_out.astype(f32)).reshape(L, 2, D_MODEL)
    deltas = jnp.abs(jnp.linspace(math.log(HY_DECAY_TARGET) / HY_SHORT_DECAY_PCT,
                                  math.log(HY_DECAY_TARGET) / HY_LONG_DECAY_PCT, D_MODEL, dtype=f32))
    h = h * jnp.exp(-t * deltas)[:, None, :]
    h = h * lax.rsqrt(jnp.sum(h * h, axis=(0, 1), keepdims=True) + NORM_EPS)
    return jnp.concatenate([h[:, 0], jnp.zeros((1, D_MODEL), f32), h[:0:-1, 1]], axis=0)

def hyena_mixer(h, w_in, b_in, short_w, short_b, f_w1, f_b1, f_w2, f_b2, f_w3, f_b3, f_wout, f_freq,
                d_bias, w_out, b_out):
    L = h.shape[1]
    u = dwconv_centred(h @ w_in + b_in, short_w, short_b)
    x0, x1, v = jnp.split(u, 3, axis=-1)
    filt = hyena_filters(L, f_w1, f_b1, f_w2, f_b2, f_w3, f_b3, f_wout, f_freq)
    z = (v * x1).astype(jnp.float32)
    zf = jnp.fft.rfft(z, n=2 * L, axis=1)
    ff = jnp.fft.rfft(filt, n=2 * L, axis=0)
    y = jnp.fft.irfft(zf * ff[None], n=2 * L, axis=1)[:, :L] + z * d_bias.astype(jnp.float32)
    return (x0 * y.astype(h.dtype)) @ w_out + b_out

def conv_ffn(h, w_up, conv_w, conv_b, w_down):
    a, g = jnp.split(h @ w_up, 2, axis=-1)
    return (a * jax.nn.gelu(dwconv_centred(g, conv_w, conv_b), approximate=False)) @ w_down

def second_inputs(seed: int = 0) -> dict:
    key = jax.random.key(seed)
    ks = iter(jax.random.split(key, 48))

    def nrm(shape, scale):
        return scale * jax.random.normal(next(ks), shape, jnp.float32)

    D = D_MODEL
    inp = {}
    inp['x'] = nrm((BATCH, SEQ, D), 1.0)
    inp['c'] = nrm((BATCH, D), 1.0)
    inp['ctx'] = nrm((BATCH, CTX_LEN, D), 1.0)
    inp['c_ctx'] = nrm((D,), 1.0)
    inp['l0_w_mod'] = nrm((D, N_MOD * D), D ** -0.5)
    inp['l0_b_mod'] = nrm((N_MOD * D,), 0.02)
    inp['l0_norm1'] = 1.0 + nrm((D,), 0.05)
    inp['l0_norm2'] = 1.0 + nrm((D,), 0.05)
    inp['l0_na_w_qkv'] = nrm((D, 3 * D), D ** -0.5)
    inp['l0_na_q_gain'] = 1.0 + nrm((NA_HEAD_DIM,), 0.05)
    inp['l0_na_k_gain'] = 1.0 + nrm((NA_HEAD_DIM,), 0.05)
    inp['l0_na_rpb'] = nrm((NA_HEADS, 2 * NA_WIN_H - 1, 2 * NA_WIN_W - 1), 0.1)
    inp['l0_na_w_o'] = nrm((D, D), D ** -0.5)
    inp['l0_ffn_w_up'] = nrm((D, 2 * D_FF_2), D ** -0.5)
    inp['l0_ffn_conv_w'] = nrm((FFN_CONV_WIDTH, D_FF_2), FFN_CONV_WIDTH ** -0.5)
    inp['l0_ffn_conv_b'] = nrm((D_FF_2,), 0.02)
    inp['l0_ffn_w_down'] = nrm((D_FF_2, D), D_FF_2 ** -0.5)
    inp['l1_w_mod'] = nrm((D, N_MOD * D), D ** -0.5)
    inp['l1_b_mod'] = nrm((N_MOD * D,), 0.02)
    inp['l1_norm1'] = 1.0 + nrm((D,), 0.05)
    inp['l1_norm2'] = 1.0 + nrm((D,), 0.05)
    inp['l1_hy_w_in'] = nrm((D, 3 * D), D ** -0.5)
    inp['l1_hy_b_in'] = nrm((3 * D,), 0.02)
    inp['l1_hy_short_w'] = nrm((HY_SHORT_WIDTH, 3 * D), HY_SHORT_WIDTH ** -0.5)
    inp['l1_hy_short_b'] = nrm((3 * D,), 0.02)
    inp['l1_hy_f_w1'] = nrm((HY_EMB_DIM, HY_FILTER_WIDTH), HY_EMB_DIM ** -0.5)
    inp['l1_hy_f_b1'] = nrm((HY_FILTER_WIDTH,), 0.1)
    inp['l1_hy_f_w2'] = nrm((HY_FILTER_WIDTH, HY_FILTER_WIDTH), HY_FILTER_WIDTH ** -0.5)
    inp['l1_hy_f_b2'] = nrm((HY_FILTER_WIDTH,), 0.1)
    inp['l1_hy_f_w3'] = nrm((HY_FILTER_WIDTH, HY_FILTER_WIDTH), HY_FILTER_WIDTH ** -0.5)
    inp['l1_hy_f_b3'] = nrm((HY_FILTER_WIDTH,), 0.1)
    inp['l1_hy_f_wout'] = nrm((HY_FILTER_WIDTH, 2 * D), HY_FILTER_WIDTH ** -0.5)
    inp['l1_hy_f_freq'] = 1.0 + nrm((HY_FILTER_WIDTH,), 0.05)
    inp['l1_hy_d_bias'] = nrm((D,), 1.0)
    inp['l1_hy_w_out'] = nrm((D, D), D ** -0.5)
    inp['l1_hy_b_out'] = nrm((D,), 0.02)
    inp['l1_ffn_w_up'] = nrm((D, 2 * D_FF_2), D ** -0.5)
    inp['l1_ffn_conv_w'] = nrm((FFN_CONV_WIDTH, D_FF_2), FFN_CONV_WIDTH ** -0.5)
    inp['l1_ffn_conv_b'] = nrm((D_FF_2,), 0.02)
    inp['l1_ffn_w_down'] = nrm((D_FF_2, D), D_FF_2 ** -0.5)
    return inp

def second_block(x, c, ctx, c_ctx,
              l0_w_mod, l0_b_mod, l0_norm1, l0_norm2, l0_na_w_qkv, l0_na_q_gain, l0_na_k_gain, l0_na_rpb,
              l0_na_w_o, l0_ffn_w_up, l0_ffn_conv_w, l0_ffn_conv_b, l0_ffn_w_down,
              l1_w_mod, l1_b_mod, l1_norm1, l1_norm2, l1_hy_w_in, l1_hy_b_in, l1_hy_short_w, l1_hy_short_b,
              l1_hy_f_w1, l1_hy_f_b1, l1_hy_f_w2, l1_hy_f_b2, l1_hy_f_w3, l1_hy_f_b3, l1_hy_f_wout, l1_hy_f_freq,
              l1_hy_d_bias, l1_hy_w_out, l1_hy_b_out, l1_ffn_w_up, l1_ffn_conv_w, l1_ffn_conv_b, l1_ffn_w_down):
    layers = [
        dict(w_mod=l0_w_mod, b_mod=l0_b_mod, norm1=l0_norm1, norm2=l0_norm2,
             mixer=(l0_na_w_qkv, l0_na_q_gain, l0_na_k_gain, l0_na_rpb, l0_na_w_o),
             ffn=(l0_ffn_w_up, l0_ffn_conv_w, l0_ffn_conv_b, l0_ffn_w_down)),
        dict(w_mod=l1_w_mod, b_mod=l1_b_mod, norm1=l1_norm1, norm2=l1_norm2,
             mixer=(l1_hy_w_in, l1_hy_b_in, l1_hy_short_w, l1_hy_short_b, l1_hy_f_w1, l1_hy_f_b1,
                    l1_hy_f_w2, l1_hy_f_b2, l1_hy_f_w3, l1_hy_f_b3, l1_hy_f_wout, l1_hy_f_freq,
                    l1_hy_d_bias, l1_hy_w_out, l1_hy_b_out),
             ffn=(l1_ffn_w_up, l1_ffn_conv_w, l1_ffn_conv_b, l1_ffn_w_down)),
    ]
    xc = ctx
    for i in range(DEPTH_2):
        p = layers[i]
        ctx_read_later = any(j % N_MIXERS == 0 for j in range(i + 1, DEPTH_2))
        sh1, sc1, g1, sh2, sc2, g2 = adaln(c[:, None, :], p['w_mod'], p['b_mod'])
        csh1, csc1, cg1, csh2, csc2, cg2 = adaln(c_ctx[None, None, :], p['w_mod'], p['b_mod'])
        h = modulate(rms_norm(x, p['norm1']), sh1, sc1)
        hc = modulate(rms_norm(xc, p['norm1']), csh1, csc1)
        if i % N_MIXERS == 0:
            w_qkv, q_gain, k_gain, rpb, w_o = p['mixer']
            w_q, w_k, w_v = jnp.split(w_qkv, 3, axis=1)
            q = rms_norm(split_heads(h @ w_q), q_gain)
            k = rms_norm(split_heads(h @ w_k), k_gain)
            v = split_heads(h @ w_v)
            kc = rms_norm(split_heads(hc @ w_k), k_gain)
            vc = split_heads(hc @ w_v)
            y = neighbourhood_attention(q, k, v, kc, vc, rpb) @ w_o
            if ctx_read_later:
                qc = rms_norm(split_heads(hc @ w_q), q_gain)
                yc = context_attention(qc, kc, vc) @ w_o
        else:
            y = hyena_mixer(h, *p['mixer'])
            if ctx_read_later:
                yc = hyena_mixer(hc, *p['mixer'])
        x = x + g1 * y
        x = x + g2 * conv_ffn(modulate(rms_norm(x, p['norm2']), sh2, sc2), *p['ffn'])
        if ctx_read_later:
            xc = xc + cg1 * yc
            xc = xc + cg2 * conv_ffn(modulate(rms_norm(xc, p['norm2']), csh2, csc2), *p['ffn'])
    return x


def setup_inputs(seed=0):
    out = dict(first_inputs(seed))
    for name, value in second_inputs(seed + 1).items():
        if name != "x":
            out[name + "_2"] = value
    return out


def reference(
    x, positions, norm_mix, w_in, conv_w, w_conv_out, ret_norm, w_ret_out, w_o, norm_mlp, w_up,
    w_down, norm_final, c_2, ctx_2, c_ctx_2, l0_w_mod_2, l0_b_mod_2, l0_norm1_2, l0_norm2_2,
    l0_na_w_qkv_2, l0_na_q_gain_2, l0_na_k_gain_2, l0_na_rpb_2, l0_na_w_o_2, l0_ffn_w_up_2,
    l0_ffn_conv_w_2, l0_ffn_conv_b_2, l0_ffn_w_down_2, l1_w_mod_2, l1_b_mod_2, l1_norm1_2,
    l1_norm2_2, l1_hy_w_in_2, l1_hy_b_in_2, l1_hy_short_w_2, l1_hy_short_b_2, l1_hy_f_w1_2,
    l1_hy_f_b1_2, l1_hy_f_w2_2, l1_hy_f_b2_2, l1_hy_f_w3_2, l1_hy_f_b3_2, l1_hy_f_wout_2,
    l1_hy_f_freq_2, l1_hy_d_bias_2, l1_hy_w_out_2, l1_hy_b_out_2, l1_ffn_w_up_2,
    l1_ffn_conv_w_2, l1_ffn_conv_b_2, l1_ffn_w_down_2,
):
    x = first_block(
        x, positions, norm_mix, w_in, conv_w, w_conv_out, ret_norm, w_ret_out, w_o, norm_mlp,
        w_up, w_down, norm_final,
    )
    return second_block(
        x, c_2, ctx_2, c_ctx_2, l0_w_mod_2, l0_b_mod_2, l0_norm1_2, l0_norm2_2, l0_na_w_qkv_2,
        l0_na_q_gain_2, l0_na_k_gain_2, l0_na_rpb_2, l0_na_w_o_2, l0_ffn_w_up_2,
        l0_ffn_conv_w_2, l0_ffn_conv_b_2, l0_ffn_w_down_2, l1_w_mod_2, l1_b_mod_2, l1_norm1_2,
        l1_norm2_2, l1_hy_w_in_2, l1_hy_b_in_2, l1_hy_short_w_2, l1_hy_short_b_2, l1_hy_f_w1_2,
        l1_hy_f_b1_2, l1_hy_f_w2_2, l1_hy_f_b2_2, l1_hy_f_w3_2, l1_hy_f_b3_2, l1_hy_f_wout_2,
        l1_hy_f_freq_2, l1_hy_d_bias_2, l1_hy_w_out_2, l1_hy_b_out_2, l1_ffn_w_up_2,
        l1_ffn_conv_w_2, l1_ffn_conv_b_2, l1_ffn_w_down_2,
    )


_drawn_inputs = setup_inputs


def setup_inputs(seed=0):
    import zlib

    import numpy as np

    out = dict(_drawn_inputs(seed))
    spreads = {}
    factors = {'ret_norm': 6.576,
     'norm_final': 2.727,
     'l0_norm1_2': 7.842,
     'l0_na_q_gain_2': 8.0,
     'l0_na_k_gain_2': 8.0,
     'l0_na_rpb_2': 8.0,
     'l0_ffn_conv_b_2': 31.567,
     'l0_norm2_2': 8.0}
    for name, (base, spread) in spreads.items():
        noise = np.random.default_rng([zlib.crc32(name.encode()), seed]).standard_normal(out[name].shape)
        drawn = base * np.exp(spread * noise) if base else spread * noise
        out[name] = __import__('jax').numpy.asarray(drawn.astype(out[name].dtype))
    for name, factor in factors.items():
        out[name] = (out[name] * factor).astype(out[name].dtype)
    return out
```

```python
from contextlib import ExitStack

import numpy as np

import concourse.bass as bass
from concourse import mybir

F32 = mybir.dt.float32
F32R = mybir.dt.float32r
I32 = mybir.dt.int32
ACT = mybir.ActivationFunctionType
ALU = mybir.AluOpType
AX_X = mybir.AxisListType.X

P = 128
D = 1024
DT = D // P
S = 512
DEPTH = 2
EPS = 1e-6
RING = 4
BLK = DT * P

RH, RQK, RV = 4, 128, 256
TOK = S // P
ROPE_BASE = 10000.0
FF = 4 * D
FF_GROUPS = FF // D

QK_JOBS = 2 * RH
V_JOBS = RH * RV // P
G_JOBS = RH * RV // P
PAIR_JOBS = 2 * DT
CONV_JOBS = 3 * DT
O_JOBS = DT
JOB_QK = 0
JOB_V = JOB_QK + QK_JOBS
JOB_G = JOB_V + V_JOBS
JOB_RET = JOB_G + G_JOBS
JOB_CONV = JOB_RET + PAIR_JOBS
JOB_MIX = JOB_CONV + CONV_JOBS
JOB_O = JOB_MIX + PAIR_JOBS
JOB_FF = JOB_O + O_JOBS
FF_GROUP_JOBS = 2 * DT
LAYER_JOBS = JOB_FF + FF_GROUPS * FF_GROUP_JOBS

TILE_H = 0
TILE_QK = TILE_H + DT
TILE_V = TILE_QK + QK_JOBS
TILE_OG = TILE_V + V_JOBS
TILE_BZ = TILE_OG + DT
TILE_MIX = TILE_BZ + DT
TILE_H2 = TILE_MIX + DT
TILE_FF = TILE_H2 + DT
LAYER_TILES = TILE_FF + FF_GROUPS * DT

EV_G = 0
EV_RET = EV_G + G_JOBS
EV_CONV = EV_RET + DT
EV_MIX = EV_CONV + DT
EV_FF = EV_MIX + DT
EV_LAYER = EV_FF + FF_GROUPS * DT

MOD_TILES = 6 * DT
MOD_LAYER = MOD_TILES // DEPTH
MOD_GROUP = MOD_LAYER // FF_GROUPS
MOD_CTX = 2 * DT * MOD_GROUP // MOD_TILES
MOD_REST = MOD_GROUP - MOD_CTX
MOD_GROUPS = MOD_TILES // MOD_GROUP
MOD_ORDER = [t for g in range(MOD_GROUPS) for t in
             [g * MOD_CTX + s for s in range(MOD_CTX)] + [2 * DT + g * MOD_REST + s for s in range(MOD_REST)]]

CTX = 256
GRID_W, GRID_H = 64, S // 64
NH, HD = 16, 64
WIN = 16
CT = CTX // P
QUARTERS = 4
QT_TILES = DT // QUARTERS
QT_HEADS = NH // QUARTERS
KEYS = 256
KEY0 = [0, 64, 192, 256]
KIND = [0, 1, 1, 2]
REAL = [slice(0, 192), slice(0, KEYS), slice(64, KEYS)]
REAL_KEYS = [s.stop - s.start for s in REAL]
MASKS = sum(REAL_KEYS)
MASK_OFF = [0, REAL_KEYS[0], REAL_KEYS[0] + REAL_KEYS[1]]
UNIT_KEYS = KEYS + CTX
BIAS_LEN = 3 * UNIT_KEYS
REACH_COLS = 32
REACH = REACH_COLS * GRID_H
TOEPLITZ_OFF = [REACH - 192, 0, 0]
V_STARTS = [0, 64, 192, 320, 384]
VA, VB, VC, VD, VE, VX0, VX1 = range(7)
V_COLS = QT_TILES * P
CHUNK_COLS = [[KEYS, KEYS + P, 64, 0], [KEYS, KEYS + P, 0, 128], [KEYS, KEYS + P, 128, 0], [KEYS, KEYS + P, 64, 128]]
SHARED_V = [VB, VD]
OWN_V = [[(VA, slice(0, 64)), (VC, slice(0, P))], [(VC, slice(0, P)), (VE, slice(64, P))]]
QT_JOBS = 3 * QT_TILES
QT_UNITS = QT_HEADS * TOK
ITEMS = 3 * QT_TILES
MASKED = 1e30
BIG = 3e38
FF2 = 2816
FF2_T = FF2 // P
FF2_GROUPS = [8, 8, 6]

ATT_JOB = DEPTH * LAYER_JOBS
ATT_ROUND = ATT_JOB // RING
WO_ROUND = ATT_ROUND + QUARTERS * QT_JOBS // RING
FF2_ROUND = WO_ROUND + DT // RING
ATT_TILE = DEPTH * LAYER_TILES
ATT_EV = DEPTH * EV_LAYER
SH1, SC1, G1, SH2, SC2, G2 = range(6)

PAR_NORM1 = 0
PAR_NORM2 = PAR_NORM1 + DT
PAR_RET = PAR_NORM2 + DT
PAR_CONV = PAR_RET + DT
PAR_LAYER = PAR_CONV + 3 * DT
PAR_FINAL = DEPTH * PAR_LAYER
PAR_N1 = PAR_FINAL + DT
PAR_N2 = PAR_N1 + DT
PAR_QG = PAR_N2 + DT
PAR_KG = PAR_QG + 1
PAR_CONV2 = PAR_KG + 1
PAR_CB2 = PAR_CONV2 + 3 * FF2_T
PAR_BMOD = PAR_CB2 + FF2_T
PAR_BCTX = PAR_BMOD + 2 * MOD_TILES
PAR_FREQ = PAR_BCTX + 4 * DT
PAR_COND = PAR_FREQ + 1
PARAMS = -(-(PAR_COND + 2 * DT) // 8) * 8

HALF_PI = float(np.pi / 2)
PI_LOW = 3.1415925
INV_2PI = float(1.0 / (2.0 * np.pi))
TWO_PI_1 = 6.28125
TWO_PI_2 = 1.9350051879882812e-03
TWO_PI_3 = float(2 * np.pi - 6.28125 - 1.9350051879882812e-03)
ROUND_MAGIC = 12582912.0


def build(nc, x, ctx_in, weights, mod_weights, params, positions, decay, key_mask, rpb, block_ones, ident, out):
    ROUNDS = weights.shape[0] // RING
    LATE = 4
    ctx = ExitStack()
    with ctx:
        sem = lambda name: ctx.enter_context(nc.semaphore(name))

        KB = 1024
        base = -(-nc.sbuf_base // 64) * 64

        def at(name, offset, shape, dt=F32):
            return nc.alloc_sbuf_tensor_at(name, [P, *shape], dt, offset=base + offset)

        def pair(name, offset):
            return (at(name + "_hi", offset, [DT, S], F32R), at(name + "_lo", offset + 16 * KB, [DT, S], F32R),
                    at(name + "_hi_f", offset, [DT, S]), at(name + "_lo_f", offset + 16 * KB, [DT, S]))

        X = at("X", 0, [DT, S])
        H_hi, H_lo, Hf, Hlf = pair("H", 16 * KB)
        A_hi, A_lo, Af, Alf = pair("A", 48 * KB)
        B_hi, B_lo, Bf, Blf = pair("B", 80 * KB)
        C_hi, C_lo, Cf, Clf = pair("C", 112 * KB)
        w_raw = at("w_raw", 144 * KB, [RING, BLK])
        w_hi = at("w_hi", 160 * KB, [RING, BLK], F32R)
        w_lo = at("w_lo", 176 * KB, [RING, BLK], F32R)
        decay_sb = at("decay_sb", 192 * KB, [RH, S])
        rope = at("rope", 200 * KB, [2, S])
        par = at("par", 204 * KB, [PARAMS])
        ones = at("ones", 204 * KB + 4 * PARAMS, [P])
        mod = at("mod", 204 * KB + 4 * PARAMS + 512, [2 * MOD_TILES])
        cond = at("cond", 204 * KB + 4 * PARAMS + 512 + 8 * MOD_TILES, [DT, 2])
        eps = at("eps", 204 * KB + 4 * PARAMS + 512 + 8 * MOD_TILES + 64, [1])
        small = at("small", 204 * KB + 4 * PARAMS + 512 + 8 * MOD_TILES + 96, [8])

        mod_ctx = at("mod_ctx", 204 * KB + 4 * PARAMS + 512 + 8 * MOD_TILES + 320, [4 * DT])

        E = at("E", 104 * KB, [4, S])
        ROOT, SUMSQ = 2, 3
        ctx_acc = at("ctx_acc", 106 * KB, [MOD_CTX, P])
        mod_w = at("mod_w", 80 * KB, [MOD_GROUP, BLK])
        ST = at("ST", 112 * KB, [3, 2, S], F32R)
        st_tmp = at("st_tmp", 124 * KB, [2, S])
        V_hi = at("V_hi", 80 * KB, [TOK, RH * RV], F32R)
        V_lo = at("V_lo", 96 * KB, [TOK, RH * RV], F32R)
        z_pos = at("z_pos", 124 * KB, [S], I32)
        z = at("z", 48 * KB, [2, S + 4])

        HC_hi = at("HC_hi", 80 * KB, [DT, CTX], F32R)
        HC_lo = at("HC_lo", 88 * KB, [DT, CTX], F32R)
        HC_lo_f = at("HC_lo_f", 88 * KB, [DT, CTX])
        ctx_sb = at("ctx_sb", 96 * KB, [DT, CTX])
        q_hi = at("q_hi", 96 * KB, [QT_TILES, S], F32R)
        q_lo = at("q_lo", 100 * KB, [QT_TILES, S], F32R)
        q_lo_f = at("q_lo_f", 100 * KB, [QT_TILES, S])
        k_hi = at("k_hi", 104 * KB, [QT_TILES * (S + CTX) + S - CTX], F32R)
        k_lo = at("k_lo", 110 * KB, [QT_TILES * (S + CTX) + S - CTX], F32R)
        k_lo_f = at("k_lo_f", 110 * KB, [QT_TILES * (S + CTX) + S - CTX])
        v_sb = at("v_sb", 116 * KB, [7, V_COLS])
        prob = at("prob", 123 * KB, [3, S])
        pt = at("pt", 129 * KB, [2, 4, 2, P])
        head_root = at("head_root", 129 * KB, [2, S])
        toeplitz = at("toeplitz", 138 * KB, [2, REACH])
        mask_sb = at("mask_sb", 140 * KB, [MASKS])
        block_sb = at("block_sb", 140 * KB + 4 * MASKS, [P])
        ident_sb = at("ident_sb", 141 * KB + 4 * MASKS, [P])
        bias = at("bias", 192 * KB, [2, BIAS_LEN])
        ctx_sq = at("ctx_sq", 116 * KB, [DT, CTX])
        ctx_sum = at("ctx_sum", 135 * KB, [CTX])
        ctx_root = at("ctx_root", 136 * KB, [CTX])
        gated = at("gated", 112 * KB, [2, S + 2])
        conv = at("conv", 120 * KB, [2, S])
        gains = at("gains", 204 * KB + 4 * PARAMS + 512 + 8 * MOD_TILES + 128, [3 * DT + 8])
        stat = at("stat", 204 * KB + 4 * PARAMS + 512 + 8 * MOD_TILES + 256, [12])

        MIN, SUM, INV, IDLE = 0, 3, 6, 9
        SCORE_BANKS, TURN_BANKS = (4, 5, 0), (6, 7, 1)

        ps = ctx.enter_context(nc.psum_tensor("ps", [P, 8, 512], F32))
        NORM_BANK, MOD_BANK, O_BANK = 4, 5, 6

        w_loaded = [sem(f"w_loaded{q}") for q in range(RING)]
        w_hi_ready = sem("w_hi_ready")
        w_lo_ready = sem("w_lo_ready")
        jobs_done = sem("jobs_done")
        bank_free = sem("bank_free")
        tiles_ready = sem("tiles_ready")
        v_banks = sem("v_banks")
        ev_ready = sem("ev_ready")
        ss_ready = sem("ss_ready")
        ms_ready = sem("ms_ready")
        rt_ready = sem("rt_ready")
        sc_ready = sem("sc_ready")
        st_ready = sem("st_ready")
        pv_done = sem("pv_done")
        o_copied = sem("o_copied")
        var_ready = sem("var_ready")
        dev_ready = sem("dev_ready")
        in_loaded = sem("in_loaded")
        par_loaded = sem("par_loaded")
        angles_ready = sem("angles_ready")
        sines_ready = sem("sines_ready")
        setup_done = sem("setup_done")
        cond_sig = sem("cond_sig")
        mod_loaded = sem("mod_loaded")
        mod_summed = sem("mod_summed")
        mod_used = sem("mod_used")
        late_loaded = sem("late_loaded")
        toep_loaded = [sem("toep_loaded0"), sem("toep_loaded1")]
        ctx_ss_ready = sem("ctx_ss_ready")
        ctx_ms_ready = sem("ctx_ms_ready")
        ctx_rt_ready = sem("ctx_rt_ready")
        hc_ready = sem("hc_ready")
        kc_mm = sem("kc_mm")
        kc_read = sem("kc_read")
        sq_ready = sem("sq_ready")
        hn_ready = sem("hn_ready")
        hn_root = sem("hn_root")
        item_ready = sem("item_ready")
        v_mm = sem("v_mm")
        v_ready = sem("v_ready")
        bias_ready = sem("bias_ready")
        s_ready = sem("s_ready")
        min_ready = sem("min_ready")
        exp_ready = sem("exp_ready")
        prob_ready = sem("prob_ready")
        turned = sem("turned")
        pt_ready = sem("pt_ready")
        o_ready = sem("o_ready")
        o_split = sem("o_split")
        conv_ready = sem("conv_ready")
        out_stored = sem("out_stored")

        block = ctx.enter_context(nc.Block())

        @block.sync
        def _(sp):
            sp.dma_start(X[:, :, :], x).then_inc(in_loaded, 16)
            for q in range(RING):
                sp.dma_start(w_raw[:, q, :], weights[q]).then_inc(w_loaded[q], 16)
            with sp.Fori(1, weights.shape[0] // RING) as i:
                for q in range(RING):
                    sp.wait_ge(w_lo_ready, i * RING + (q - RING + 1))
                    sp.dma_start(w_raw[:, q, :], weights[i * RING + q]).then_inc(w_loaded[q], 16)

            for m in range(DT):
                sp.wait_ge(bank_free, ROUNDS * RING - DT + RING + m + 1)
                sp.dma_start(out[:, m, :], X[:, m, :]).then_inc(out_stored, 16)
            sp.wait_ge(out_stored, 16 * DT)

        @block.gpsimd
        def _(pool):
            def low(n, q):
                pool.wait_ge(w_hi_ready, n + 1)
                nc.gpsimd.tensor_tensor(w_lo[:, q, :], w_raw[:, q, :], w_hi[:, q, :].bitcast(F32),
                                        ALU.subtract).then_inc(w_lo_ready, 1)

            def low_rounds(first, last):
                with pool.Fori(first, last) as i:
                    for q in range(RING):
                        low(i * RING + q, q)

            low_rounds(0, ATT_ROUND)
            pool.wait_ge(late_loaded, 16 * LATE)
            with pool.Fori(0, QUARTERS // 2) as b:
                for half in range(2):
                    for s in range(QT_JOBS):
                        low(b * (2 * QT_JOBS) + (ATT_JOB + half * QT_JOBS + s), (half * QT_JOBS + s) % RING)
                    for hh in range(QT_HEADS):
                        head = b * (2 * QT_HEADS) + (half * QT_HEADS + hh)
                        side = hh % 2
                        pool.wait_ge(toep_loaded[side], (b * QT_HEADS + (half * QT_HEADS + hh) // 2 + 1) * 16)
                        pool.wait_ge(min_ready, head * TOK + TOK)
                        for kind in range(3):
                            n = REAL_KEYS[kind]
                            o = kind * UNIT_KEYS + REAL[kind].start
                            t = TOEPLITZ_OFF[kind]
                            last = nc.gpsimd.tensor_tensor(
                                bias[:, side, o:o + n], mask_sb[:, MASK_OFF[kind]:MASK_OFF[kind] + n],
                                toeplitz[:, side, t:t + n], ALU.subtract)
                        last.then_inc(bias_ready, 1)
            low_rounds(WO_ROUND, ROUNDS)

        @block.tensor
        def _(pe):
            def product(dst, w, xs, start, stop):
                for a, (l, r) in enumerate(((0, 0), (0, 1), (1, 0))):
                    mm = nc.tensor.matmul(dst, w[l], xs[r], start=start and a == 0, stop=stop and a == 2)
                return mm

            def job(n, q, hi, lo, tiles, kt=DT):
                pe.wait_ge(w_lo_ready, n + 1)
                pe.wait_ge(bank_free, n + 1)
                for k in range(kt):
                    if tiles is not None:
                        pe.wait_ge(tiles_ready, tiles + (k + 1))
                    mm = product(ps[:, q, :], (w_hi[:, q, k * P:(k + 1) * P], w_lo[:, q, k * P:(k + 1) * P]),
                                 (hi[:, k, :], lo[:, k, :]), k == 0, k == kt - 1)
                mm.then_inc(jobs_done, 1)

            def jobs(n0, count, hi, lo, tiles, kt=DT, before=None):
                with pe.Fori(0, count // RING) as i:
                    for q in range(RING):
                        if before is not None and q == 0:
                            pe.wait_ge(*before)
                        job(n0 + i * RING + q, q, hi, lo, tiles, kt)

            def norm_sum(v):
                pe.wait_ge(ss_ready, v + 1)
                nc.tensor.matmul(ps[:, NORM_BANK, :], ones[:, :], E[:, SUMSQ, :], start=True,
                                 stop=True).then_inc(ms_ready, 1)

            def value_jobs(n0, tiles):
                for i in range(V_JOBS // RING):
                    pe.wait_ge(w_lo_ready, n0 + (i + 1) * RING)
                    for t in range(TOK):
                        n = n0 + i * RING + t
                        pe.wait_ge(bank_free, n + 1)
                        for k in range(DT):
                            mm = product(
                                ps[:, t, :],
                                (H_hi[:, k, t * P:(t + 1) * P], H_lo[:, k, t * P:(t + 1) * P]),
                                [w[:, :, k * P:(k + 1) * P] for w in (w_hi, w_lo)], k == 0, k == DT - 1)
                        if t < TOK - 1:
                            mm.then_inc(v_banks, 1)
                    mm.then_inc(jobs_done, RING)

            def attention(L):
                pe.wait_ge(tiles_ready, L * LAYER_TILES + TILE_OG)

                def scores(u):
                    h, j = divmod(u, TOK)
                    if u >= 2:
                        pe.wait_ge(st_ready, L * 16 + (u - 1))
                    k_tile = slice(j * P, (j + 1) * P)
                    product(ps[:, 4 + u % 2, 0:S - j * P], (A_hi[:, RH + h, k_tile], A_lo[:, RH + h, k_tile]),
                            (A_hi[:, h, j * P:S], A_lo[:, h, j * P:S]), True, True).then_inc(sc_ready, 1)

                def values(u):
                    h, j = divmod(u, TOK)
                    pe.wait_ge(st_ready, L * 16 + (u + 1))
                    if j == 0 and h:
                        pe.wait_ge(o_copied, L * RH + h)
                    n = S - j * P
                    for t in range(2):
                        v = slice((2 * h + t) * P, (2 * h + t + 1) * P)
                        mm = product(ps[:, O_BANK + t, j * P:S], (V_hi[:, j, v], V_lo[:, j, v]),
                                     (ST[:, u % 3, 0, 0:n], ST[:, u % 3, 1, 0:n]), j == 0, j == TOK - 1)
                    mm.then_inc(pv_done, 1)

                def variance(h):
                    pe.wait_ge(o_copied, L * RH + (h + 1))
                    nc.tensor.matmul(ps[:, h, :], ones[:, :], Alf[:, h, :], start=True, stop=False)
                    nc.tensor.matmul(ps[:, h, :], ones[:, :], Alf[:, RH + h, :], start=False,
                                     stop=True).then_inc(var_ready, 1)

                units = RH * TOK
                scores(0)
                for u in range(units):
                    if u + 1 < units:
                        scores(u + 1)
                    values(u)
                    if u % TOK == 1 and u > TOK:
                        variance(u // TOK - 1)
                variance(RH - 1)

            pe.sem_inc(jobs_done, RING)
            pe.sem_inc(bank_free, RING)
            pe.sem_inc(mod_used, 1)
            pe.wait_ge(setup_done, 1)

            with pe.Fori(0, DEPTH) as L:
                n = L * LAYER_JOBS
                tiles = L * LAYER_TILES
                norm_sum(2 * L)
                jobs(n + JOB_QK, QK_JOBS, H_hi, H_lo, tiles + TILE_H)
                value_jobs(n + JOB_V, tiles + TILE_H)
                attention(L)
                jobs(n + JOB_G, G_JOBS, H_hi, H_lo, tiles + TILE_H, before=(dev_ready, L * RH + RH))
                with pe.Fori(0, PAIR_JOBS // RING) as i:
                    for q in range(RING):
                        if q % 2 == 0:
                            job(n + JOB_RET + i * RING + q, q, H_hi, H_lo, tiles + TILE_H)
                        else:
                            job(n + JOB_RET + i * RING + q, q, C_hi, C_lo, tiles + TILE_OG)
                jobs(n + JOB_CONV, CONV_JOBS, H_hi, H_lo, tiles + TILE_H)
                with pe.Fori(0, PAIR_JOBS // RING) as i:
                    for q in range(RING):
                        if q % 2 == 0:
                            job(n + JOB_MIX + i * RING + q, q, H_hi, H_lo, tiles + TILE_H)
                        else:
                            job(n + JOB_MIX + i * RING + q, q, B_hi, B_lo, tiles + TILE_BZ)
                jobs(n + JOB_O, O_JOBS, A_hi, A_lo, tiles + TILE_MIX)
                norm_sum(2 * L + 1)
                with pe.Fori(0, FF_GROUPS // 2) as g2:
                    for half, (hi, lo) in enumerate(((A_hi, A_lo), (C_hi, C_lo))):
                        g = g2 * 2 + half
                        ng = n + JOB_FF + g2 * (2 * FF_GROUP_JOBS) + half * FF_GROUP_JOBS
                        jobs(ng, DT, H_hi, H_lo, tiles + TILE_H2)
                        jobs(ng + DT, DT, hi, lo, tiles + TILE_FF + g2 * (2 * DT) + half * DT)
                        pe.wait_ge(mod_summed, L * FF_GROUPS + g + 1)
                        for s in range(MOD_GROUP):
                            nc.tensor.matmul(ps[:, MOD_BANK, bass.ds((g * MOD_GROUP + s) * 2, 2)], mod_w[:, s, 0:P],
                                             ones[:, 0:2], start=True, stop=True)
                        for s in range(MOD_CTX):
                            mm = nc.tensor.matmul(ps[:, MOD_BANK, bass.ds((g * MOD_CTX + s + MOD_LAYER) * 2, 2)],
                                                  ctx_acc[:, s, :], ones[:, 0:2], start=True, stop=True)
                        mm.then_inc(mod_used, 1)

            norm_sum(2 * DEPTH)
            norm_sum(2 * DEPTH + 1)
            pe.wait_ge(ctx_ss_ready, 1)
            nc.tensor.matmul(ps[:, MOD_BANK, 0:CTX], ones[:, :], ctx_sum[:, :], start=True,
                             stop=True).then_inc(ctx_ms_ready, 1)

            def quarter(b, half):
                n0 = b * (2 * QT_JOBS) + (ATT_JOB + half * QT_JOBS)
                item0 = b * (2 * ITEMS) + half * ITEMS

                def slot(s):
                    return (half * QT_JOBS + s) % RING

                def head_sums(i):
                    width = CTX if i in (2, 4) else S
                    pe.wait_ge(sq_ready, item0 + (i + 1))
                    if i >= 2:
                        pe.wait_ge(hn_root, item0 + (i - 1))
                    nc.tensor.matmul(ps[:, 4 + i % 2, 0:width], block_sb[:, :], prob[:, i % 2, 0:width],
                                     start=True, stop=True).then_inc(hn_ready, 1)

                def ctx_keys(s, t):
                    q = slot(s)
                    pe.wait_ge(w_lo_ready, n0 + (s + 1))
                    for k in range(DT):
                        pe.wait_ge(hc_ready, k + 1)
                        mm = product(ps[:, 6 + t, 0:CTX],
                                     (w_hi[:, q, k * P:(k + 1) * P], w_lo[:, q, k * P:(k + 1) * P]),
                                     (HC_hi[:, k, :], HC_lo[:, k, :]), k == 0, k == DT - 1)
                    mm.then_inc(kc_mm, 1)

                def values():
                    pe.wait_ge(w_lo_ready, n0 + QT_JOBS)
                    pe.wait_ge(item_ready, item0 + 2)
                    q = slot(2 * QT_TILES)
                    for tile in range(7):
                        if tile == 4:
                            pe.wait_ge(hn_root, item0 + ITEMS)
                            pe.wait_ge(kc_read, (b * 2 + half) * QT_TILES + 2)
                        for k in range(DT):
                            if tile < len(V_STARTS):
                                toks = slice(V_STARTS[tile], V_STARTS[tile] + P)
                                w = (H_hi[:, k, toks], H_lo[:, k, toks])
                            else:
                                toks = slice((tile - 5) * P, (tile - 4) * P)
                                w = (HC_hi[:, k, toks], HC_lo[:, k, toks])
                            mm = product(ps[:, 4 + tile // 2, (tile % 2) * V_COLS:(tile % 2 + 1) * V_COLS], w,
                                         [x[:, q:q + 2, k * P:(k + 1) * P] for x in (w_hi, w_lo)], k == 0, k == DT - 1)
                        if tile % 2:
                            mm.then_inc(v_mm, 1)
                    mm.then_inc(jobs_done, 2)

                tiles = ATT_TILE
                job(n0, slot(0), H_hi, H_lo, tiles)
                job(n0 + 1, slot(1), H_hi, H_lo, tiles)
                head_sums(0)
                ctx_keys(2, 0)
                head_sums(1)
                job(n0 + 2, slot(2), H_hi, H_lo, tiles)
                head_sums(2)
                ctx_keys(3, 1)
                head_sums(3)
                job(n0 + 3, slot(3), H_hi, H_lo, tiles)
                head_sums(4)
                head_sums(5)
                pe.wait_ge(hn_root, item0 + ITEMS)
                values()

                unit0 = (b * 2 + half) * QT_UNITS
                head0 = (b * 2 + half) * QT_HEADS
                pe.wait_ge(item_ready, item0 + ITEMS)
                pe.wait_ge(v_ready, (b * 2 + half) * 4 + 4)

                def scores(u):
                    hh, i = divmod(u, TOK)
                    t, rows = hh // 2, slice(HD * (hh % 2), HD * (hh % 2) + HD)
                    qs = (q_hi[rows, t, i * P:(i + 1) * P], q_lo[rows, t, i * P:(i + 1) * P])
                    step = S - KEY0[i]
                    first = t * (S + CTX) + KEY0[i]
                    ks = [x[rows, first:first + 2 * step].rearrange("p (a n) -> p a n", n=step)[:, :, 0:KEYS]
                          for x in (k_hi, k_lo)]
                    product(ps[:, SCORE_BANKS[u % 3], :], qs, ks, True, True).then_inc(s_ready, 1)

                def turn(u):
                    pe.wait_ge(prob_ready, unit0 + (u + 1))
                    for c, at_col in enumerate(CHUNK_COLS[u % TOK]):
                        mm = nc.tensor.transpose(ps[:, TURN_BANKS[u % 3], c * P:(c + 1) * P],
                                                 prob[:, u % 3, at_col:at_col + P], ident_sb[:, :])
                    mm.then_inc(turned, 1)

                def weigh(pair_):
                    hh, side = divmod(pair_, TOK // 2)
                    cols = slice((hh // 2) * P, (hh // 2 + 1) * P)
                    pe.wait_ge(pt_ready, unit0 + 2 * pair_ + 2)
                    if side == 0 and hh >= 2:
                        pe.wait_ge(o_split, head0 + (hh - 1))
                    o0 = side * 2 * P
                    buf = pair_ % 2
                    for c, tile in enumerate((VX0, VX1, SHARED_V[side])):
                        nc.tensor.matmul(ps[:, 2 + hh % 2, o0:o0 + 2 * P], v_sb[:, tile, cols],
                                         pt[:, buf, c, :, :].rearrange("p t n -> p (t n)"), start=c == 0, stop=False)
                    for t, (tile, rows) in enumerate(OWN_V[side]):
                        mm = nc.tensor.matmul(ps[:, 2 + hh % 2, o0 + t * P:o0 + (t + 1) * P], v_sb[rows, tile, cols],
                                              pt[rows, buf, 3, t, :], start=False, stop=t == 1)
                    if side == TOK // 2 - 1:
                        mm.then_inc(o_ready, 1)

                scores(0)
                scores(1)
                for u in range(QT_UNITS):
                    if u + 2 < QT_UNITS:
                        scores(u + 2)
                    turn(u)
                    if u and u % 2 == 0:
                        weigh(u // 2 - 1)
                weigh(QT_UNITS // 2 - 1)
                pe.wait_ge(o_split, head0 + QT_HEADS)

            with pe.Fori(0, QUARTERS // 2) as b:
                for half in range(2):
                    quarter(b, half)
            jobs(WO_ROUND * RING, DT, A_hi, A_lo, None)
            norm_sum(2 * DEPTH + 2)
            n, tile = FF2_ROUND * RING, ATT_TILE + 2 * DT
            for g, kt in enumerate(FF2_GROUPS):
                hi, lo = ((A_hi, A_lo), (B_hi, B_lo))[g % 2]
                jobs(n, 2 * kt, H_hi, H_lo, ATT_TILE + DT)
                jobs(n + 2 * kt, DT, hi, lo, tile, kt)
                n += 2 * kt + DT
                tile += kt


        @block.scalar
        def _(act):
            act.dma_start(par[:, :], params).then_inc(par_loaded, 16)
            act.dma_start(z_pos[:, :], positions).then_inc(par_loaded, 16)
            act.dma_start(decay_sb[:, :, :], decay).then_inc(par_loaded, 16)

            def ahead(r, q):
                s = (q + RING - 1) % RING
                m = r if q == 0 else r + 1
                if isinstance(m, int) and m >= ROUNDS:
                    return
                act.wait_ge(w_loaded[s], (m + 1) * 16)
                act.wait_ge(jobs_done, m * RING + (s + 1))
                nc.scalar.activation(w_hi[:, s, :], w_raw[:, s, :], ACT.Copy).then_inc(w_hi_ready, 1)

            def phase(r0, rounds, epilogue=None, per_body=1):
                with act.Fori(0, rounds // per_body) as i:
                    for s in range(per_body * RING):
                        r, q = r0 + i * per_body + s // RING, s % RING
                        ahead(r, q)
                        if epilogue is not None:
                            epilogue(r, i, s)

            def evacuate(r, q, func, dst):
                act.wait_ge(jobs_done, r * RING + (q + 1 + RING))
                nc.scalar.activation(dst, ps[:, q, :], func).then_inc(ev_ready, 1)

            def gates(dst):
                def epilogue(r, i, s):
                    if s % 2 == 0:
                        evacuate(r, s, ACT.Sigmoid, dst[:, s, :])
                return epilogue

            def root(v):
                act.wait_ge(ms_ready, v + 1)
                nc.scalar.activation(E[:, ROOT, :], ps[:, NORM_BANK, :], ACT.Sqrt, bias=eps[:, :],
                                     scale=1.0 / D).then_inc(rt_ready, 1)

            act.wait_ge(angles_ready, 1)
            nc.scalar.activation(rope[:, 0, :], Cf[:, 4, :], ACT.Sin).then_inc(sines_ready, 1)
            nc.scalar.activation(rope[:, 1, :], Cf[:, 5, :], ACT.Sin).then_inc(sines_ready, 1)
            nc.scalar.activation(cond[:, :, :], par[:, PAR_COND:PAR_COND + 2 * DT], ACT.Sigmoid).then_inc(cond_sig, 1)
            for q in range(RING - 1):
                act.wait_ge(w_loaded[q], 16)
                nc.scalar.activation(w_hi[:, q, :], w_raw[:, q, :], ACT.Copy).then_inc(w_hi_ready, 1)

            with act.Fori(0, DEPTH) as L:
                r = L * (LAYER_JOBS // RING)
                root(2 * L)
                phase(r + JOB_QK // RING, (QK_JOBS + V_JOBS) // RING)
                for h in range(RH):
                    act.wait_ge(pv_done, L * (RH * TOK) + TOK * (h + 1))
                    for t in range(2):
                        nc.scalar.activation(Clf[:, 2 * h + t, :], ps[:, O_BANK + t, :], ACT.Copy)
                        sq = nc.scalar.activation(Alf[:, h + RH * t, :], ps[:, O_BANK + t, :], ACT.Square)
                    sq.then_inc(o_copied, 1)
                    act.wait_ge(var_ready, L * RH + (h + 1))
                    nc.scalar.activation(Af[:, h, :], ps[:, h, :], ACT.Sqrt, bias=eps[:, :],
                                         scale=1.0 / RV).then_inc(dev_ready, 1)
                phase(r + JOB_G // RING, G_JOBS // RING,
                      lambda r, i, s: evacuate(r, s, ACT.Sigmoid, Bf[:, s, :]))
                phase(r + JOB_RET // RING, PAIR_JOBS // RING, gates(Bf))

                def conv_in(r, i, s):
                    if s % 3 == 0:
                        evacuate(r, s % RING, ACT.Copy, Cf[:, s % RING, :])
                phase(r + JOB_CONV // RING, CONV_JOBS // RING, conv_in, per_body=3)
                phase(r + JOB_MIX // RING, PAIR_JOBS // RING, gates(Cf))
                phase(r + JOB_O // RING, O_JOBS // RING)
                root(2 * L + 1)
                with act.Fori(0, FF_GROUPS) as g:
                    rg = r + JOB_FF // RING + g * (FF_GROUP_JOBS // RING)
                    act.wait_ge(mod_used, L * FF_GROUPS + g + 1)
                    act.dma_start(mod_w[:, :, :], mod_weights[L * FF_GROUPS + g]).then_inc(mod_loaded, 16)
                    phase(rg, DT // RING, lambda r, i, s: evacuate(r, s, ACT.Relu, E[:, s, :]))
                    phase(rg + DT // RING, DT // RING)

            act.wait_ge(jobs_done, ATT_JOB + RING)
            act.wait_ge(mod_used, DEPTH * FF_GROUPS + 1)
            act.dma_start(ctx_sb[:, :, :], ctx_in).then_inc(late_loaded, 16)
            act.dma_start(mask_sb[:, :], key_mask).then_inc(late_loaded, 16)
            act.dma_start(block_sb[:, :], block_ones).then_inc(late_loaded, 16)
            act.dma_start(ident_sb[:, :], ident).then_inc(late_loaded, 16)
            for side in range(2):
                act.dma_start(toeplitz[:, side, :], rpb[side]).then_inc(toep_loaded[side], 16)
            root(2 * DEPTH)
            root(2 * DEPTH + 1)
            act.wait_ge(ctx_ms_ready, 1)
            nc.scalar.activation(ctx_root[:, :], ps[:, MOD_BANK, 0:CTX], ACT.Sqrt, bias=eps[:, :],
                                 scale=1.0 / D).then_inc(ctx_rt_ready, 1)

            def quarter(b, half):
                r0 = b * (2 * QT_JOBS // RING) + ATT_ROUND
                item0 = b * (2 * ITEMS) + half * ITEMS
                unit0 = (b * 2 + half) * QT_UNITS

                def place(s):
                    n = half * QT_JOBS + s
                    return r0 + n // RING, n % RING

                def squares(i):
                    s, is_ctx = ((0, False), (1, False), (2, True), (2, False), (3, True), (3, False))[i]
                    if is_ctx:
                        t = s - 2
                        act.wait_ge(kc_mm, (b * 2 + half) * QT_TILES + (t + 1))
                        src, width = ps[:, 6 + t, 0:CTX], CTX
                    else:
                        r, q = place(s)
                        act.wait_ge(jobs_done, r * RING + (q + 1 + RING))
                        src, width = ps[:, q, :], S
                    if i >= 2:
                        act.wait_ge(hn_ready, item0 + (i - 1))
                    nc.scalar.activation(prob[:, i % 2, 0:width], src, ACT.Square).then_inc(sq_ready, 1)

                def head_roots(i):
                    width = CTX if i in (2, 4) else S
                    act.wait_ge(hn_ready, item0 + (i + 1))
                    if i >= 2:
                        act.wait_ge(item_ready, item0 + (i - 1))
                    nc.scalar.activation(head_root[:, i % 2, 0:width], ps[:, 4 + i % 2, 0:width], ACT.Sqrt,
                                         bias=eps[:, :], scale=1.0 / HD).then_inc(hn_root, 1)

                def exponentials(u):
                    s = u % 3
                    act.wait_ge(min_ready, unit0 + (u + 1 + 2 * TOK))
                    nc.scalar.activation(prob[:, s, :], prob[:, s, :], ACT.Exp,
                                         bias=stat[:, MIN + s:MIN + s + 1], scale=-1.0,
                                         accum_out=stat[:, SUM + s:SUM + s + 1]).then_inc(exp_ready, 1)

                def copy_turned(u):
                    act.wait_ge(turned, unit0 + (u + 1))
                    nc.scalar.activation(pt[:, (u // 2) % 2, :, u % 2, :],
                                         ps[:, TURN_BANKS[u % 3], :].rearrange("p (c n) -> p c n", n=P),
                                         ACT.Copy).then_inc(pt_ready, 1)

                ahead(*place(0))
                squares(0)
                ahead(*place(1))
                squares(1)
                head_roots(0)
                squares(2)
                head_roots(1)
                ahead(*place(2))
                squares(3)
                head_roots(2)
                squares(4)
                head_roots(3)
                squares(5)
                head_roots(4)
                head_roots(5)
                for s in (3, 4, 5):
                    ahead(*place(s))
                exponentials(0)
                exponentials(1)
                for u in range(QT_UNITS):
                    if u + 2 < QT_UNITS:
                        exponentials(u + 2)
                    copy_turned(u)
                    if u % TOK == TOK - 1:
                        head = b * (2 * QT_HEADS) + (half * QT_HEADS + u // TOK)
                        side = (u // TOK) % 2
                        act.wait_ge(bias_ready, head + 1)
                        act.dma_start(toeplitz[:, side, :], rpb[head + 2]).then_inc(toep_loaded[side], 16)

            with act.Fori(0, QUARTERS // 2) as b:
                for half in range(2):
                    quarter(b, half)
            phase(WO_ROUND, DT // RING)
            root(2 * DEPTH + 2)
            r, m0 = FF2_ROUND, 0
            for g, kt in enumerate(FF2_GROUPS):
                def gate(r, i, s):
                    if s % 2:
                        return
                    t = s // 2
                    act.wait_ge(jobs_done, r * RING + (s + 1 + RING))
                    nc.scalar.activation(gated[:, t, 1:S + 1], ps[:, s, :], ACT.Copy).then_inc(ev_ready, 1)
                    m = i * 2 + (m0 + t)
                    act.wait_ge(conv_ready, m + 1)
                    nc.scalar.activation(conv[:, t, :], conv[:, t, :], ACT.Gelu,
                                         bias=par[:, bass.ds(m + PAR_CB2, 1)]).then_inc(ev_ready, 1)
                phase(r, 2 * kt // RING, gate)
                if g < len(FF2_GROUPS) - 1:
                    phase(r + 2 * kt // RING, DT // RING)
                else:
                    for k in range(DT):
                        ahead(ROUNDS - DT // RING + k // RING, k % RING)
                r += (2 * kt + DT) // RING
                m0 += kt
            act.wait_ge(toep_loaded[0], 16 * (NH // 2 + 1))
            act.wait_ge(toep_loaded[1], 16 * (NH // 2 + 1))


        @block.vector
        def _(dve):
            fence = dve.drain
            V = nc.vector

            def split(whole, hi, lo, ready=tiles_ready):
                fence()
                V.tensor_copy(hi, whole)
                fence()
                V.tensor_tensor(lo, whole, hi.bitcast(F32), ALU.subtract).then_inc(ready, 1)

            def column(base, L, m=0):
                return par[:, bass.ds(L * PAR_LAYER + m + base, 1)]

            def job_done(r, q):
                dve.wait_ge(jobs_done, r * RING + (q + 1 + RING))

            def sum_squares(m, first):
                fence()
                V.tensor_tensor(E[:, 0, :], X[:, m, :], X[:, m, :], ALU.mult)
                fence()
                if first:
                    return V.tensor_copy(E[:, SUMSQ, :], E[:, 0, :])
                return V.tensor_tensor(E[:, SUMSQ, :], E[:, SUMSQ, :], E[:, 0, :], ALU.add)

            def norm(v, gain):
                dve.wait_ge(rt_ready, v + 1)
                V.reciprocal(E[:, ROOT, :], E[:, ROOT, :])
                fence()
                for m in range(DT):
                    V.scalar_tensor_tensor(out=Hlf[:, m, :], in0=X[:, m, :], scalar=gain(m),
                                           in1=E[:, ROOT, :], op0=ALU.mult, op1=ALU.mult)
                    split(Hlf[:, m, :], H_hi[:, m, :], H_lo[:, m, :])

            def add_to_stream(r, i, q, squares=False, first=False):
                job_done(r, q)
                m = i * RING + q
                add = V.tensor_tensor(X[:, m, :], X[:, m, :], ps[:, q, :], ALU.add)
                add.then_inc(bank_free, 1)
                if squares:
                    return sum_squares(m, first)

            V.memset(ones[:, :], 1.0)
            V.memset(eps[:, :], EPS)
            dve.wait_ge(in_loaded, 16)
            for m in range(DT):
                last = sum_squares(m, m == 0)
            last.then_inc(ss_ready, 1)
            dve.wait_ge(par_loaded, 48)
            V.tensor_copy(Cf[:, 0, :], z_pos[:, :])
            fence()
            V.tensor_scalar(Cf[:, 0, :], Cf[:, 0, :], par[:, PAR_FREQ:PAR_FREQ + 1], None, ALU.mult)
            for which, shift in ((0, 0.25), (1, 0.0)):
                fence()
                V.tensor_scalar(Cf[:, 1, :], Cf[:, 0, :], INV_2PI, shift, ALU.mult, ALU.add)
                fence()
                V.tensor_scalar(Cf[:, 1, :], Cf[:, 1, :], ROUND_MAGIC, None, ALU.add)
                fence()
                V.tensor_scalar(Cf[:, 1, :], Cf[:, 1, :], -ROUND_MAGIC, None, ALU.add)
                fence()
                V.scalar_tensor_tensor(out=Cf[:, 2, :], in0=Cf[:, 1, :], scalar=-TWO_PI_1, in1=Cf[:, 0, :],
                                       op0=ALU.mult, op1=ALU.add)
                fence()
                V.scalar_tensor_tensor(out=Cf[:, 3, :], in0=Cf[:, 1, :], scalar=-TWO_PI_2, in1=Cf[:, 2, :],
                                       op0=ALU.mult, op1=ALU.add)
                fence()
                V.scalar_tensor_tensor(out=Cf[:, 2, :], in0=Cf[:, 1, :], scalar=-TWO_PI_3, in1=Cf[:, 3, :],
                                       op0=ALU.mult, op1=ALU.add)
                fence()
                if which == 0:
                    V.tensor_scalar(Cf[:, 2, :], Cf[:, 2, :], HALF_PI, None, ALU.add)
                    fence()
                done_angle = V.tensor_scalar(Cf[:, 4 + which, :], Cf[:, 2, :], PI_LOW, -PI_LOW, ALU.min, ALU.max)
            done_angle.then_inc(angles_ready, 1)
            dve.wait_ge(sines_ready, 2)
            V.tensor_scalar(rope[P // 2:P, 1, :], rope[P // 2:P, 1, :], -1.0, None, ALU.mult)
            dve.wait_ge(cond_sig, 1)
            V.tensor_tensor(cond[:, :, :].rearrange("p k c -> p (k c)"), cond[:, :, :].rearrange("p k c -> p (k c)"),
                            par[:, PAR_COND:PAR_COND + 2 * DT], ALU.mult)
            dve.drain().then_inc(setup_done, 1)

            with dve.Fori(0, DEPTH) as L:
                r = L * (LAYER_JOBS // RING)
                norm(2 * L, lambda m: column(PAR_NORM1 + m, L))

                with dve.Fori(0, QK_JOBS // RING) as i:
                    for q in range(RING):
                        job_done(r + JOB_QK // RING + i, q)
                        half = P // 2
                        V.tensor_tensor(Cf[:, 0, :], ps[:, q, :], rope[:, 0, :], ALU.mult)
                        V.tensor_tensor(Cf[half:P, 1, :], ps[0:half, q, :], rope[0:half, 1, :], ALU.mult)
                        V.tensor_tensor(Cf[0:half, 1, :], ps[half:P, q, :], rope[half:P, 1, :],
                                        ALU.mult).then_inc(bank_free, 1)
                        fence()
                        m = i * RING + q
                        V.tensor_tensor(Alf[:, m, :], Cf[:, 0, :], Cf[:, 1, :], ALU.add)
                        split(Alf[:, m, :], A_hi[:, m, :], A_lo[:, m, :])

                for i in range(V_JOBS // RING):
                    for t in range(TOK):
                        if t < TOK - 1:
                            dve.wait_ge(v_banks, (L * (V_JOBS // RING) + i) * (TOK - 1) + (t + 1))
                        else:
                            job_done(r + (JOB_V // RING + i), t)
                        bank = ps[:, t, :].rearrange("p (h v) -> p h v", v=RV)
                        V.tensor_reduce(small[:, 0:2], bank, AX_X, ALU.add)
                        fence()
                        V.tensor_scalar(small[:, 2:4], small[:, 0:2], -1.0 / RV, None, ALU.mult)
                        fence()
                        for h in range(2):
                            last = V.tensor_scalar(Cf[:, 0, h * RV:(h + 1) * RV], bank[:, h, :],
                                                   small[:, 2 + h:3 + h], None, ALU.add)
                        last.then_inc(bank_free, 1)
                        cols = slice(i * 512, (i + 1) * 512)
                        split(Cf[:, 0, :], V_hi[:, t, cols], V_lo[:, t, cols])

                for u in range(RH * TOK):
                    h, j = divmod(u, TOK)
                    n = S - j * P
                    dve.wait_ge(sc_ready, L * (RH * TOK) + (u + 1))
                    if u >= 3:
                        dve.wait_ge(pv_done, L * (RH * TOK) + (u - 2))
                    V.tensor_tensor(st_tmp[:, u % 2, 0:n], ps[:, 4 + u % 2, 0:n], decay_sb[:, h, 0:n], ALU.mult)
                    split(st_tmp[:, u % 2, 0:n], ST[:, u % 3, 0, 0:n], ST[:, u % 3, 1, 0:n], st_ready)

                for i in range(G_JOBS // RING):
                    for q in range(RING):
                        m = i * RING + q
                        if m % 2 == 0:
                            dve.wait_ge(dev_ready, L * RH + (m // 2 + 1))
                            V.reciprocal(Af[:, m // 2, :], Af[:, m // 2, :])
                        fence()
                        dve.wait_ge(ev_ready, L * EV_LAYER + (EV_G + m + 1))
                        V.tensor_tensor(Bf[:, 4, :], Bf[:, q, :], ps[:, q, :], ALU.mult).then_inc(bank_free, 1)
                        V.scalar_tensor_tensor(out=Bf[:, 5, :], in0=Clf[:, m, :], scalar=column(PAR_RET + m, L),
                                               in1=Af[:, m // 2, :], op0=ALU.mult, op1=ALU.mult)
                        fence()
                        V.tensor_tensor(Clf[:, m, :], Bf[:, 4, :], Bf[:, 5, :], ALU.mult)
                        split(Clf[:, m, :], C_hi[:, m, :], C_lo[:, m, :])

                with dve.Fori(0, PAIR_JOBS // RING) as i:
                    for q in range(0, RING, 2):
                        dve.wait_ge(ev_ready, L * EV_LAYER + i * 2 + (EV_RET + q // 2 + 1))
                        job_done(r + JOB_RET // RING + i, q + 1)
                        V.tensor_tensor(Alf[:, i * 2 + q // 2, :], Bf[:, q, :], ps[:, q + 1, :],
                                        ALU.mult).then_inc(bank_free, 2)

                V.memset(z[:, :, 0:2], 0.0)
                with dve.Fori(0, DT // RING) as i:
                    for t in range(RING):
                        s = 3 * t
                        rs = lambda s: r + JOB_CONV // RING + i * 3 + s // RING
                        m = i * RING + t
                        dve.wait_ge(ev_ready, L * EV_LAYER + i * RING + (EV_CONV + t + 1))
                        job_done(rs(s + 1), (s + 1) % RING)
                        V.tensor_tensor(z[:, t % 2, 2:S + 2], Cf[:, s % RING, :], ps[:, (s + 1) % RING, :],
                                        ALU.mult).then_inc(bank_free, 2)
                        fence()
                        V.tensor_scalar(Cf[:, 4, :], z[:, t % 2, 2:S + 2], column(PAR_CONV + 2 * DT, L, m), None, ALU.mult)
                        fence()
                        V.scalar_tensor_tensor(out=Cf[:, 5, :], in0=z[:, t % 2, 1:S + 1],
                                               scalar=column(PAR_CONV + DT, L, m), in1=Cf[:, 4, :],
                                               op0=ALU.mult, op1=ALU.add)
                        fence()
                        V.scalar_tensor_tensor(out=Cf[:, 4, :], in0=z[:, t % 2, 0:S],
                                               scalar=column(PAR_CONV, L, m), in1=Cf[:, 5, :],
                                               op0=ALU.mult, op1=ALU.add)
                        fence()
                        job_done(rs(s + 2), (s + 2) % RING)
                        V.tensor_tensor(Blf[:, m, :], Cf[:, 4, :], ps[:, (s + 2) % RING, :],
                                        ALU.mult).then_inc(bank_free, 1)
                        split(Blf[:, m, :], B_hi[:, m, :], B_lo[:, m, :])

                with dve.Fori(0, PAIR_JOBS // RING) as i:
                    for q in range(0, RING, 2):
                        m = i * 2 + q // 2
                        dve.wait_ge(ev_ready, L * EV_LAYER + i * 2 + (EV_MIX + q // 2 + 1))
                        job_done(r + JOB_MIX // RING + i, q + 1)
                        V.tensor_tensor(Cf[:, 4, :], Cf[:, q, :], ps[:, q + 1, :], ALU.mult).then_inc(bank_free, 2)
                        fence()
                        V.tensor_tensor(Alf[:, m, :], Cf[:, 4, :], Alf[:, m, :], ALU.add)
                        split(Alf[:, m, :], A_hi[:, m, :], A_lo[:, m, :])

                for i in range(O_JOBS // RING):
                    for q in range(RING):
                        last = add_to_stream(r + (JOB_O // RING + i), i, q, True, i == 0 and q == 0)
                last.then_inc(ss_ready, 1)
                norm(2 * L + 1, lambda m: column(PAR_NORM2 + m, L))

                def ff_up(n_ev, hi, lo, lo_f):
                    with dve.Fori(0, DT // RING) as i:
                        for q in range(RING):
                            m = i * RING + q
                            dve.wait_ge(ev_ready, n_ev + i * RING + (q + 1))
                            V.tensor_tensor(lo_f[:, m, :], E[:, q, :], ps[:, q, :], ALU.mult).then_inc(bank_free, 1)
                            split(lo_f[:, m, :], hi[:, m, :], lo[:, m, :])

                def ff_down(rg, last_group):
                    if not last_group:
                        with dve.Fori(0, DT // RING) as i:
                            for q in range(RING):
                                add_to_stream(rg + i, i, q)
                        return
                    for i in range(DT // RING):
                        for q in range(RING):
                            last = add_to_stream(rg + i, i, q, True, i == 0 and q == 0)
                    last.then_inc(ss_ready, 1)

                def mod_sums(g):
                    dve.wait_ge(mod_loaded, (L * FF_GROUPS + g + 1) * 16)
                    for who, tiles, acc in ((1, MOD_CTX, ctx_acc[:, :, :]), (0, MOD_GROUP, mod_w[:, :, 0:P])):
                        V.tensor_scalar(acc, mod_w[:, 0:tiles, 0:P], cond[:, 0, who:who + 1], None, ALU.mult)
                        for k in range(1, DT):
                            fence()
                            last = V.scalar_tensor_tensor(out=acc, in0=mod_w[:, 0:tiles, k * P:(k + 1) * P],
                                                          scalar=cond[:, k, who:who + 1], in1=acc,
                                                          op0=ALU.mult, op1=ALU.add)
                    last.then_inc(mod_summed, 1)

                for g in range(FF_GROUPS):
                    rg = r + (JOB_FF + g * FF_GROUP_JOBS) // RING
                    ff_up(L * EV_LAYER + (EV_FF + g * DT),
                          *((A_hi, A_lo, Alf) if g % 2 == 0 else (C_hi, C_lo, Clf)))
                    mod_sums(g)
                    ff_down(rg + DT // RING, g == FF_GROUPS - 1)

                dve.wait_ge(mod_used, L * FF_GROUPS + (FF_GROUPS + 1))
                lanes = L * (2 * MOD_LAYER)
                V.tensor_tensor(mod[:, bass.ds(lanes, 2 * MOD_LAYER)], ps[:, MOD_BANK, 0:2 * MOD_LAYER],
                                par[:, bass.ds(lanes + PAR_BMOD, 2 * MOD_LAYER)], ALU.add)
                lanes = L * (2 * DT)
                V.tensor_tensor(mod_ctx[:, bass.ds(lanes, 2 * DT)], ps[:, MOD_BANK, 2 * MOD_LAYER:2 * MOD_LAYER + 2 * DT],
                                par[:, bass.ds(lanes + PAR_BCTX, 2 * DT)], ALU.add)

            def by_column(ap):
                return ap.rearrange("p (r c) -> p c r", c=GRID_W)

            def in_columns(ap):
                return ap.rearrange("p (c r) -> p c r", r=GRID_H)

            by_group = mod[:, :].rearrange("p (g s w) -> p g s w", s=MOD_GROUP, w=2)

            def vector(which, m=0, who=0):
                if who:
                    return mod_ctx[:, (which * DT + m) * 2:(which * DT + m) * 2 + 1]
                at_tile = MOD_ORDER.index(which * DT + m)
                return mod[:, at_tile * 2:at_tile * 2 + 1]

            def all_of(which, who=0):
                if who:
                    return mod_ctx[:, 2 * which * DT:2 * (which + 1) * DT].rearrange(
                        "p (g s w) -> p g s w", s=MOD_CTX, w=2)[:, :, :, 0]
                if which < 2:
                    g = which * DT // MOD_CTX
                    return by_group[:, g:g + DT // MOD_CTX, 0:MOD_CTX, 0]
                g = (which - 2) * DT // MOD_REST
                return by_group[:, g:g + DT // MOD_REST, MOD_CTX:, 0]

            for a, (which, who, gain) in enumerate(((SC1, 0, PAR_N1), (SC1, 1, PAR_N1), (SC2, 0, PAR_N2))):
                fence()
                tiles = MOD_CTX if which < 2 else MOD_REST
                V.scalar_tensor_tensor(out=gains[:, a * DT:(a + 1) * DT].rearrange("p (g s) -> p g s", s=tiles),
                                       in0=all_of(which, who), scalar=1.0,
                                       in1=par[:, gain:gain + DT].rearrange("p (g s) -> p g s", s=tiles),
                                       op0=ALU.add, op1=ALU.mult)
            V.tensor_scalar(gains[:, 3 * DT:3 * DT + 1], par[:, PAR_QG:PAR_QG + 1], -HD ** -0.5, None, ALU.mult)

            dve.wait_ge(rt_ready, 2 * DEPTH + 1)
            V.reciprocal(E[:, ROOT, :], E[:, ROOT, :])
            fence()
            for m in range(DT):
                V.scalar_tensor_tensor(out=X[:, m, :], in0=X[:, m, :], scalar=par[:, PAR_FINAL + m:PAR_FINAL + m + 1],
                                       in1=E[:, ROOT, :], op0=ALU.mult, op1=ALU.mult)
                last = sum_squares(m, m == 0)
            last.then_inc(ss_ready, 1)
            dve.wait_ge(late_loaded, 16 * LATE)
            V.tensor_tensor(ctx_sq[:, :, :].rearrange("p k t -> p (k t)"), ctx_sb[:, :, :].rearrange("p k t -> p (k t)"),
                            ctx_sb[:, :, :].rearrange("p k t -> p (k t)"), ALU.mult)
            fence()
            V.tensor_reduce(ctx_sum[:, :], ctx_sq[:, :, :].rearrange("p k t -> p t k"), AX_X,
                            ALU.add).then_inc(ctx_ss_ready, 1)
            V.memset(bias[:, :, :], 0.0)
            fence()
            V.memset(bias[:, :, REAL[0].stop:KEYS], MASKED)
            V.memset(bias[:, :, 2 * UNIT_KEYS:2 * UNIT_KEYS + REAL[2].start], MASKED)
            dve.drain()
            dve.sem_inc(min_ready, 2 * TOK)

            def adaptive(v, gain0, shift, columns_order):
                dve.wait_ge(rt_ready, v + 1)
                V.reciprocal(E[:, ROOT, :], E[:, ROOT, :])
                fence()
                for m in range(DT):
                    src, rstd, dst = X[:, m, :], E[:, ROOT, :], Hlf[:, m, :]
                    if columns_order:
                        src, rstd, dst = by_column(src), by_column(rstd), in_columns(dst)
                    V.scalar_tensor_tensor(out=dst, in0=src, scalar=gains[:, gain0 + m:gain0 + m + 1], in1=rstd,
                                           op0=ALU.mult, op1=ALU.mult)
                    fence()
                    V.tensor_scalar(Hlf[:, m, :], Hlf[:, m, :], vector(shift, m), None, ALU.add)
                    split(Hlf[:, m, :], H_hi[:, m, :], H_lo[:, m, :])

            adaptive(2 * DEPTH + 1, 0, SH1, True)
            dve.wait_ge(ctx_rt_ready, 1)
            V.reciprocal(ctx_root[:, :], ctx_root[:, :])
            fence()
            for m in range(DT):
                V.scalar_tensor_tensor(out=HC_lo_f[:, m, :], in0=ctx_sb[:, m, :], scalar=gains[:, DT + m:DT + m + 1],
                                       in1=ctx_root[:, :], op0=ALU.mult, op1=ALU.mult)
                fence()
                V.tensor_scalar(HC_lo_f[:, m, :], HC_lo_f[:, m, :], vector(SH1, m, 1), None, ALU.add)
                split(HC_lo_f[:, m, :], HC_hi[:, m, :], HC_lo[:, m, :], hc_ready)

            def quarter(b, half):
                r0 = b * (2 * QT_JOBS // RING) + ATT_ROUND
                item0 = b * (2 * ITEMS) + half * ITEMS
                unit0 = (b * 2 + half) * QT_UNITS
                q_gain, k_gain = gains[:, 3 * DT:3 * DT + 1], par[:, PAR_KG:PAR_KG + 1]

                def item(i):
                    s, is_ctx = ((0, False), (1, False), (2, True), (2, False), (3, True), (3, False))[i]
                    t = s % 2
                    width = CTX if is_ctx else S
                    first = t * (S + CTX) + (S if is_ctx else 0)
                    whole, hi, lo = ([a[:, t, :] for a in (q_lo_f, q_hi, q_lo)] if s < 2 else
                                     [a[:, first:first + width] for a in (k_lo_f, k_hi, k_lo)])
                    n = half * QT_JOBS + s
                    src = ps[:, 6 + t, 0:CTX] if is_ctx else ps[:, n % RING, :]
                    dve.wait_ge(hn_root, item0 + (i + 1))
                    V.reciprocal(head_root[:, i % 2, 0:width], head_root[:, i % 2, 0:width])
                    fence()
                    mul = V.scalar_tensor_tensor(out=whole, in0=src, scalar=q_gain if s < 2 else k_gain,
                                                 in1=head_root[:, i % 2, 0:width], op0=ALU.mult, op1=ALU.mult)
                    mul.then_inc(kc_read if is_ctx else bank_free, 1)
                    split(whole, hi, lo, item_ready)

                def least(u):
                    hh, i = divmod(u, TOK)
                    s, o = u % 3, KIND[i] * UNIT_KEYS
                    if i == 0:
                        dve.wait_ge(bias_ready, (b * 2 + half) * QT_HEADS + (hh + 1))
                    dve.wait_ge(s_ready, unit0 + (u + 1))
                    V.memset(stat[:, IDLE + s:IDLE + s + 1], 0.0)
                    V.tensor_tensor_reduce(prob[:, s, :], ps[:, SCORE_BANKS[s], :], bias[:, hh % 2, o:o + UNIT_KEYS],
                                           1.0, BIG, ALU.add, ALU.min, stat[:, MIN + s:MIN + s + 1]).then_inc(min_ready, 1)

                def divide(u):
                    s = u % 3
                    dve.wait_ge(exp_ready, unit0 + (u + 1))
                    V.reciprocal(stat[:, INV + s:INV + s + 1], stat[:, SUM + s:SUM + s + 1])
                    fence()
                    V.tensor_scalar(prob[:, s, :], prob[:, s, :], stat[:, INV + s:INV + s + 1], None,
                                    ALU.mult).then_inc(prob_ready, 1)

                def output(hh):
                    rows = slice(HD * (hh % 2), HD * (hh % 2) + HD)
                    m = (b * 2 + half) * QT_TILES + hh // 2
                    dve.wait_ge(o_ready, (b * 2 + half) * QT_HEADS + (hh + 1))
                    V.tensor_copy(A_hi[rows, m, :], ps[rows, 2 + hh % 2, :])
                    fence()
                    V.tensor_tensor(A_lo[rows, m, :], ps[rows, 2 + hh % 2, :], A_hi[rows, m, :].bitcast(F32),
                                    ALU.subtract).then_inc(o_split, 1)

                for i in range(ITEMS):
                    item(i)
                for pair_ in range(4):
                    first, count = 2 * pair_, 2 if pair_ < 3 else 1
                    n = count * V_COLS
                    if pair_ < 3:
                        dve.wait_ge(v_mm, (b * 2 + half) * 3 + (pair_ + 1))
                    else:
                        dve.wait_ge(jobs_done, (b * 2 + half) * QT_JOBS + (ATT_JOB + QT_JOBS + RING))
                    V.tensor_copy(v_sb[:, first:first + count, :].rearrange("p a v -> p (a v)"),
                                  ps[:, 4 + pair_, 0:n]).then_inc(v_ready, 1)
                dve.drain().then_inc(bank_free, 2)

                least(0)
                least(1)
                divide(0)
                for u in range(QT_UNITS):
                    if u + 2 < QT_UNITS:
                        least(u + 2)
                    if u + 1 < QT_UNITS:
                        divide(u + 1)
                    if u % TOK == 2 and u > TOK:
                        output(u // TOK - 1)
                output(QT_HEADS - 1)

            with dve.Fori(0, QUARTERS // 2) as b:
                for half in range(2):
                    quarter(b, half)

            for i in range(DT // RING):
                for q in range(RING):
                    m = i * RING + q
                    job_done(WO_ROUND + i, q)
                    V.scalar_tensor_tensor(out=by_column(X[:, m, :]), in0=in_columns(ps[:, q, :]), scalar=vector(G1, m),
                                           in1=by_column(X[:, m, :]), op0=ALU.mult, op1=ALU.add).then_inc(bank_free, 1)
                    last = sum_squares(m, m == 0)
            last.then_inc(ss_ready, 1)
            V.memset(gated[:, :, 0:1], 0.0)
            V.memset(gated[:, :, S + 1:S + 2], 0.0)
            adaptive(2 * DEPTH + 2, 2 * DT, SH2, False)

            r, m0 = FF2_ROUND, 0
            for g, kt in enumerate(FF2_GROUPS):
                hi, lo, lo_f = ((A_hi, A_lo, Alf), (B_hi, B_lo, Blf))[g % 2]
                with dve.Fori(0, 2 * kt // RING) as i:
                    for t in range(2):
                        m = i * 2 + (m0 + t)
                        col = lambda tap: par[:, bass.ds(m + (PAR_CONV2 + tap * FF2_T), 1)]
                        fence()
                        dve.wait_ge(ev_ready, m * 2 + (ATT_EV + 1))
                        V.tensor_scalar(conv[:, t, :], gated[:, t, 1:S + 1], col(1), None, ALU.mult)
                        fence()
                        V.scalar_tensor_tensor(out=conv[:, t, :], in0=gated[:, t, 0:S], scalar=col(0), in1=conv[:, t, :],
                                               op0=ALU.mult, op1=ALU.add)
                        fence()
                        V.scalar_tensor_tensor(out=conv[:, t, :], in0=gated[:, t, 2:S + 2], scalar=col(2),
                                               in1=conv[:, t, :], op0=ALU.mult, op1=ALU.add).then_inc(conv_ready, 1)
                        dve.wait_ge(ev_ready, m * 2 + (ATT_EV + 2))
                        job_done(r + i, 2 * t + 1)
                        k = i * 2 + t
                        V.tensor_tensor(lo_f[:, k, :], conv[:, t, :], ps[:, 2 * t + 1, :], ALU.mult).then_inc(bank_free, 2)
                        split(lo_f[:, k, :], hi[:, k, :], lo[:, k, :])
                r += 2 * kt // RING
                m0 += kt
                for i in range(DT // RING):
                    for q in range(RING):
                        m = i * RING + q
                        job_done(r + i, q)
                        add = V.scalar_tensor_tensor(out=X[:, m, :], in0=ps[:, q, :], scalar=vector(G2, m),
                                                     in1=X[:, m, :], op0=ALU.mult, op1=ALU.add)
                        add.then_inc(bank_free, 1)
                r += DT // RING



def tiles_of(w):
    k, m = w.shape
    return w.reshape(k // P, P, m // P, P).transpose(2, 1, 0, 3).reshape(m // P, P, k)


def columns(v):
    return np.ascontiguousarray(v.reshape(-1, P).T)


def hybrid_stream(w_in, w_conv_out, w_ret_out, w_o, w_up, w_down):
    t = tiles_of(w_in)
    conv_b, conv_c, conv_u = t[0:DT], t[DT:2 * DT], t[2 * DT:3 * DT]
    at = 3 * DT
    qk = t[at:at + QK_JOBS]
    v = t[at + QK_JOBS:at + QK_JOBS + V_JOBS]
    g = t[at + QK_JOBS + V_JOBS:at + QK_JOBS + V_JOBS + G_JOBS]
    gate_a, gate_b = t[-2 * DT:-DT], t[-DT:]
    both = lambda *parts: np.stack(parts, 1).reshape(-1, P, D)
    blocks = [qk, v, g, both(gate_b, tiles_of(w_ret_out)), both(conv_c, conv_u, conv_b),
              both(gate_a, tiles_of(w_conv_out)), tiles_of(w_o)]
    for i in range(FF_GROUPS):
        blocks += [tiles_of(w_up[:, i * D:(i + 1) * D]), tiles_of(w_down[i * D:(i + 1) * D])]
    return np.concatenate(blocks)


def decay_table():
    log_gamma = np.log1p(-np.exp2(-5.0 - np.arange(RH)))
    rel = np.arange(S)[None, :] - np.arange(P)[:, None]
    t = np.where(rel >= 0, np.exp(log_gamma[:, None, None] * np.maximum(rel, 0)), 0.0) * RQK ** -0.5
    return np.ascontiguousarray(t.transpose(1, 0, 2).astype(np.float32))


def stream_of_features(x):
    return np.ascontiguousarray(x.T.reshape(-1, P, x.shape[0]).transpose(1, 0, 2))


def attention_stream(w_qkv, w_o, w_up, w_down):
    q, k, v = (tiles_of(w_qkv[:, i * D:(i + 1) * D]) for i in range(3))
    up = tiles_of(w_up)
    a, g = up[:FF2_T], up[FF2_T:]
    blocks = []
    for i in range(QUARTERS):
        t = slice(i * QT_TILES, (i + 1) * QT_TILES)
        blocks += [q[t], k[t], v[t]]
    blocks.append(tiles_of(w_o))
    m = 0
    for kt in FF2_GROUPS:
        blocks.append(np.stack([g[m:m + kt], a[m:m + kt]], 1).reshape(-1, P, D))
        down = tiles_of(w_down[m * P:(m + kt) * P])
        blocks.append(np.pad(down, ((0, 0), (0, 0), (0, D - down.shape[2]))))
        m += kt
    return np.concatenate(blocks)


def key_masks():
    masks = []
    for tile, kind in ((0, 0), (1, 1), (3, 2)):
        qc = tile * (P // GRID_H) + np.arange(P) // GRID_H
        kc = (KEY0[tile] + np.arange(KEYS)) // GRID_H
        first = np.clip(qc - WIN // 2, 0, GRID_W - WIN)[:, None]
        masks.append(np.where((kc >= first) & (kc < first + WIN), 0.0, MASKED)[:, REAL[kind]])
    return np.concatenate(masks, 1).astype(np.float32)


def toeplitz_biases(rpb):
    reach_left = WIN // 2
    cq, rq = np.arange(P) // GRID_H, np.arange(P) % GRID_H
    cl, rk = np.arange(REACH) // GRID_H - reach_left, np.arange(REACH) % GRID_H
    wide = np.pad(rpb, ((0, 2), (0, 0), (P // GRID_H, P // GRID_H + REACH_COLS)))
    dr = rk[None, :] - rq[:, None] + GRID_H - 1
    dc = cl[None, :] - cq[:, None] + WIN - 1 + P // GRID_H
    return np.ascontiguousarray(wide[:, dr, dc])


def parameters(a):
    layers = [np.concatenate([columns(a["norm_mix"][l]), columns(a["norm_mlp"][l]), columns(a["ret_norm"][l]),
                              columns(a["conv_w"][l].reshape(-1))], 1) for l in range(DEPTH)]
    half = RQK // 2
    freq = (np.float32(ROPE_BASE) ** (-np.arange(half, dtype=np.float32) / np.float32(half))).astype(np.float32)
    cond = np.stack([columns(a["c_2"][0]), columns(a["c_ctx_2"])], 2).reshape(P, -1)
    parts = layers + [
        columns(a["norm_final"]), columns(a["l0_norm1_2"]), columns(a["l0_norm2_2"]),
        np.tile(a["l0_na_q_gain_2"], 2)[:, None], np.tile(a["l0_na_k_gain_2"], 2)[:, None],
        columns(a["l0_ffn_conv_w_2"].reshape(-1)), columns(a["l0_ffn_conv_b_2"]),
        np.repeat(columns(a["l0_b_mod_2"])[:, MOD_ORDER], 2, axis=1),
        np.repeat(columns(a["l0_b_mod_2"])[:, :2 * DT], 2, axis=1), np.tile(freq, 2)[:, None], cond]
    p = np.concatenate(parts, 1)
    return np.pad(p, ((0, 0), (0, PARAMS - p.shape[1])))


def kernel(**inputs):
    import concourse.bacc as bacc
    from concourse.bass_utils import run_bass_kernel_spmd

    a = {k: np.asarray(v) for k, v in inputs.items()}
    blocks = [hybrid_stream(*(a[n][l] for n in ("w_in", "w_conv_out", "w_ret_out", "w_o", "w_up", "w_down")))
              for l in range(DEPTH)]
    blocks.append(attention_stream(a["l0_na_w_qkv_2"], a["l0_na_w_o_2"], a["l0_ffn_w_up_2"], a["l0_ffn_w_down_2"]))
    mod_blocks = tiles_of(a["l0_w_mod_2"])[MOD_ORDER].reshape(-1, MOD_GROUP, P, D).transpose(0, 2, 1, 3)
    head_rows = np.arange(P) // HD
    arrays = {
        "x": stream_of_features(a["x"][0]),
        "context": stream_of_features(a["ctx_2"][0]),
        "weights": np.concatenate(blocks),
        "mod_weights": np.ascontiguousarray(mod_blocks),
        "params": parameters(a),
        "positions": np.ascontiguousarray(np.broadcast_to(a["positions"], (P, S))),
        "decay": decay_table(),
        "key_mask": key_masks(),
        "biases": toeplitz_biases(a["l0_na_rpb_2"]),
        "block_ones": (head_rows[:, None] == head_rows[None, :]).astype(np.float32),
        "identity": np.eye(P, dtype=np.float32),
    }
    nc = bacc.Bacc("TRN2", target_bir_lowering=False, num_devices=1)
    args = [nc.dram_tensor(name, v.shape, mybir.dt.from_np(v.dtype), kind="ExternalInput").ap()
            for name, v in arrays.items()]
    out = nc.dram_tensor("out", (P, DT, S), F32, kind="ExternalOutput").ap()
    build(nc, *args, out)
    got = run_bass_kernel_spmd(nc, [arrays], core_ids=[0]).results[0]["out"]
    return np.ascontiguousarray(got.transpose(2, 1, 0).reshape(1, S, D))
```

```python
from contextlib import ExitStack

import numpy as np

import concourse.bass as bass
from concourse import mybir

F32 = mybir.dt.float32
F32R = mybir.dt.float32r
I32 = mybir.dt.int32
ACT = mybir.ActivationFunctionType
ALU = mybir.AluOpType
AX_X = mybir.AxisListType.X

P = 128
D = 1024
DT = D // P
S = 512
DEPTH = 2
EPS = 1e-6
RING = 4
BLK = DT * P

RH, RQK, RV = 4, 128, 256
TOK = S // P
ROPE_BASE = 10000.0
FF = 4 * D
FF_GROUPS = FF // D
V_WIDE = 512
V_TILES = D // V_WIDE

QK_JOBS = 2 * RH
V_JOBS = RH * RV // P
G_JOBS = RH * RV // P
PAIR_JOBS = 2 * DT
CONV_JOBS = 3 * DT
O_JOBS = DT
JOB_V = 0
JOB_QK = JOB_V + V_JOBS
JOB_G = JOB_QK + QK_JOBS
JOB_RET = JOB_G + G_JOBS
JOB_CONV = JOB_RET + PAIR_JOBS
JOB_MIX = JOB_CONV + CONV_JOBS
JOB_O = JOB_MIX + PAIR_JOBS
JOB_FF = JOB_O + O_JOBS
FF_GROUP_JOBS = 2 * DT
LAYER_JOBS = JOB_FF + FF_GROUPS * FF_GROUP_JOBS

TILE_H = 0
TILE_V = TILE_H + DT
TILE_QK = TILE_V + V_JOBS
TILE_OG = TILE_QK + QK_JOBS
TILE_BZ = TILE_OG + DT
TILE_MIX = TILE_BZ + DT
TILE_H2 = TILE_MIX + DT
TILE_FF = TILE_H2 + DT
LAYER_TILES = TILE_FF + FF_GROUPS * DT

EV_G = 0
EV_RET = EV_G + G_JOBS
EV_CONV = EV_RET + DT
EV_MIX = EV_CONV + DT
EV_FF = EV_MIX + DT
EV_LAYER = EV_FF + FF_GROUPS * DT

MOD_TILES = 6 * DT
MOD_LAYER = MOD_TILES // DEPTH
MOD_GROUP = MOD_LAYER // FF_GROUPS
MOD_CTX = 2 * DT * MOD_GROUP // MOD_TILES
MOD_REST = MOD_GROUP - MOD_CTX
MOD_GROUPS = MOD_TILES // MOD_GROUP
MOD_ORDER = [t for g in range(MOD_GROUPS) for t in
             [g * MOD_CTX + s for s in range(MOD_CTX)] + [2 * DT + g * MOD_REST + s for s in range(MOD_REST)]]

CTX = 256
GRID_W, GRID_H = 64, S // 64
NH, HD = 16, 64
WIN = 16
QUARTERS = 4
QT_TILES = DT // QUARTERS
QT_HEADS = NH // QUARTERS
KEYS = 256
KEY0 = [0, 64, 192, 256]
KIND = [0, 1, 1, 2]
REAL = [slice(0, 192), slice(0, KEYS), slice(64, KEYS)]
REAL_KEYS = [s.stop - s.start for s in REAL]
MASKS = sum(REAL_KEYS)
MASK_OFF = [0, REAL_KEYS[0], REAL_KEYS[0] + REAL_KEYS[1]]
UNIT_KEYS = KEYS + CTX
BIAS_LEN = 3 * UNIT_KEYS
REACH_COLS = 32
REACH = REACH_COLS * GRID_H
TOEPLITZ_OFF = [REACH - 192, 0, 0]
V_STARTS = [0, 64, 192, 320, 384]
VA, VB, VC, VD, VE, VX0, VX1 = range(7)
V_COLS = QT_TILES * P
CHUNK_COLS = [[KEYS, KEYS + P, 64, 0], [KEYS, KEYS + P, 0, 128], [KEYS, KEYS + P, 128, 0], [KEYS, KEYS + P, 64, 128]]
SHARED_V = [VB, VD]
OWN_V = [[(VA, slice(0, 64)), (VC, slice(0, P))], [(VC, slice(0, P)), (VE, slice(64, P))]]
QT_JOBS = 3 * QT_TILES
QT_UNITS = QT_HEADS * TOK
ITEMS = 3 * QT_TILES
MASKED = 1e30
BIG = 3e38
FF2 = 2816
FF2_T = FF2 // P
FF2_GROUPS = [8, 8, 6]

ATT_JOB = DEPTH * LAYER_JOBS
ATT_ROUND = ATT_JOB // RING
WO_ROUND = ATT_ROUND + QUARTERS * QT_JOBS // RING
FF2_ROUND = WO_ROUND + DT // RING
ATT_TILE = DEPTH * LAYER_TILES
ATT_EV = DEPTH * EV_LAYER
SH1, SC1, G1, SH2, SC2, G2 = range(6)

PAR_NORM1 = 0
PAR_NORM2 = PAR_NORM1 + DT
PAR_RET = PAR_NORM2 + DT
PAR_CONV = PAR_RET + DT
PAR_LAYER = PAR_CONV + 3 * DT
PAR_FINAL = DEPTH * PAR_LAYER
PAR_N1 = PAR_FINAL + DT
PAR_N2 = PAR_N1 + DT
PAR_QG = PAR_N2 + DT
PAR_KG = PAR_QG + 1
PAR_CONV2 = PAR_KG + 1
PAR_CB2 = PAR_CONV2 + 3 * FF2_T
PAR_BMOD = PAR_CB2 + FF2_T
PAR_BCTX = PAR_BMOD + 2 * MOD_TILES
PAR_FREQ = PAR_BCTX + 4 * DT
PAR_COND = PAR_FREQ + 1
PARAMS = -(-(PAR_COND + 2 * DT) // 8) * 8

HALF_PI = float(np.pi / 2)
PI_LOW = 3.1415925
INV_2PI = float(1.0 / (2.0 * np.pi))
TWO_PI_1 = 6.28125
TWO_PI_2 = 1.9350051879882812e-03
TWO_PI_3 = float(2 * np.pi - 6.28125 - 1.9350051879882812e-03)
ROUND_MAGIC = 12582912.0


def build(nc, x, ctx_in, weights, mod_weights, params, positions, decay, key_mask, rpb, block_ones, ident, out):
    ROUNDS = weights.shape[0] // RING
    X_PARTS, X_PART = DT // 2, 2
    LATE = 3
    ctx = ExitStack()
    with ctx:
        sem = lambda name: ctx.enter_context(nc.semaphore(name))

        KB = 1024
        base = -(-nc.sbuf_base // 64) * 64

        def at(name, offset, shape, dt=F32):
            return nc.alloc_sbuf_tensor_at(name, [P, *shape], dt, offset=base + offset)

        def pair(name, offset):
            return (at(name + "_hi", offset, [DT, S], F32R), at(name + "_lo", offset + 16 * KB, [DT, S], F32R),
                    at(name + "_hi_f", offset, [DT, S]), at(name + "_lo_f", offset + 16 * KB, [DT, S]))

        X = at("X", 0, [DT, S])
        H_hi, H_lo, Hf, Hlf = pair("H", 16 * KB)
        A_hi, A_lo, Af, Alf = pair("A", 48 * KB)
        B_hi, B_lo, Bf, Blf = pair("B", 80 * KB)
        C_hi, C_lo, Cf, Clf = pair("C", 112 * KB)
        w_raw = at("w_raw", 144 * KB, [RING, BLK])
        w_hi = at("w_hi", 160 * KB, [RING, BLK], F32R)
        w_lo = at("w_lo", 176 * KB, [RING, BLK], F32R)
        decay_sb = at("decay_sb", 192 * KB, [RH, S])
        rope = at("rope", 200 * KB, [2, S])
        par = at("par", 204 * KB, [PARAMS])
        ones = at("ones", 204 * KB + 4 * PARAMS, [P])
        mod = at("mod", 204 * KB + 4 * PARAMS + 512, [2 * MOD_TILES])
        cond = at("cond", 204 * KB + 4 * PARAMS + 512 + 8 * MOD_TILES, [DT, 2])
        eps = at("eps", 204 * KB + 4 * PARAMS + 512 + 8 * MOD_TILES + 64, [1])
        small = at("small", 204 * KB + 4 * PARAMS + 512 + 8 * MOD_TILES + 96, [8])

        mod_ctx = at("mod_ctx", 204 * KB + 4 * PARAMS + 512 + 8 * MOD_TILES + 320, [4 * DT])

        E = at("E", 104 * KB, [4, S])
        ROOT, SUMSQ = 2, 3
        ctx_acc = at("ctx_acc", 106 * KB, [MOD_CTX, P])
        mod_w = at("mod_w", 80 * KB, [MOD_GROUP, BLK])
        ST = at("ST", 112 * KB, [3, 2, S], F32R)
        st_tmp = at("st_tmp", 124 * KB, [2, S])
        V_hi = at("V_hi", 80 * KB, [TOK, RH * RV], F32R)
        V_lo = at("V_lo", 96 * KB, [TOK, RH * RV], F32R)
        z_pos = at("z_pos", 124 * KB, [S], I32)
        z = at("z", 48 * KB, [2, S + 4])

        HC_hi = at("HC_hi", 80 * KB, [DT, CTX], F32R)
        HC_lo = at("HC_lo", 88 * KB, [DT, CTX], F32R)
        HC_lo_f = at("HC_lo_f", 88 * KB, [DT, CTX])
        ctx_sb = at("ctx_sb", 48 * KB, [DT, CTX])
        q_hi = at("q_hi", 96 * KB, [QT_TILES, S], F32R)
        q_lo = at("q_lo", 100 * KB, [QT_TILES, S], F32R)
        q_lo_f = at("q_lo_f", 100 * KB, [QT_TILES, S])
        k_hi = at("k_hi", 104 * KB, [QT_TILES * (S + CTX) + S - CTX], F32R)
        k_lo = at("k_lo", 110 * KB, [QT_TILES * (S + CTX) + S - CTX], F32R)
        k_lo_f = at("k_lo_f", 110 * KB, [QT_TILES * (S + CTX) + S - CTX])
        v_sb = at("v_sb", 116 * KB, [7, V_COLS])
        prob = at("prob", 123 * KB, [3, S])
        pt = at("pt", 129 * KB, [2, 4, 2, P])
        head_root = at("head_root", 129 * KB, [2, S])
        vt = at("vt", 133 * KB, [QT_TILES, S])
        vt_ctx = at("vt_ctx", 127 * KB, [QT_TILES, CTX])
        toeplitz = at("toeplitz", 138 * KB, [2, REACH])
        mask_sb = at("mask_sb", 140 * KB, [MASKS])
        block_sb = at("block_sb", 140 * KB + 4 * MASKS, [P])
        ident_sb = at("ident_sb", 141 * KB + 4 * MASKS, [P])
        bias = at("bias", 192 * KB, [2, BIAS_LEN])
        ctx_sq = at("ctx_sq", 56 * KB, [DT, CTX])
        ctx_sum = at("ctx_sum", 64 * KB, [CTX])
        ctx_root = at("ctx_root", 65 * KB, [CTX])
        gated = at("gated", 112 * KB, [2, S + 2])
        conv = at("conv", 120 * KB, [2, S])
        gains = at("gains", 204 * KB + 4 * PARAMS + 512 + 8 * MOD_TILES + 128, [3 * DT + 8])
        stat = at("stat", 204 * KB + 4 * PARAMS + 512 + 8 * MOD_TILES + 256, [12])

        MIN, SUM, INV, IDLE = 0, 3, 6, 9
        SCORE_BANKS, TURN_BANKS = (4, 5, 0), (6, 7, 1)

        ps = ctx.enter_context(nc.psum_tensor("ps", [P, 8, 512], F32))
        NORM_BANK, MOD_BANK = 4, 5
        RET_BANKS, VAR_BANK = (4, 5, 1), 0
        O_BANKS = (6, 2)

        w_loaded = [sem(f"w_loaded{q}") for q in range(RING)]
        w_hi_ready = sem("w_hi_ready")
        w_lo_ready = sem("w_lo_ready")
        jobs_done = sem("jobs_done")
        bank_free = sem("bank_free")
        tiles_ready = sem("tiles_ready")
        ev_ready = sem("ev_ready")
        ss_ready = sem("ss_ready")
        ms_ready = sem("ms_ready")
        rt_ready = sem("rt_ready")
        h_scaled = sem("h_scaled")
        h_high = sem("h_high")
        sc_ready = sem("sc_ready")
        st_ready = sem("st_ready")
        pv_done = sem("pv_done")
        o_copied = sem("o_copied")
        var_ready = sem("var_ready")
        dev_ready = sem("dev_ready")
        x_loaded = [sem(f"x_loaded{j}") for j in range(X_PARTS)]
        x_squared = sem("x_squared")
        ctx_loaded = sem("ctx_loaded")
        ctx_squared = sem("ctx_squared")
        xn_ready = sem("xn_ready")
        xn_squared = sem("xn_squared")
        par_loaded = sem("par_loaded")
        decay_loaded = sem("decay_loaded")
        angles_ready = sem("angles_ready")
        sines_ready = sem("sines_ready")
        cond_sig = sem("cond_sig")
        mod_loaded = sem("mod_loaded")
        mod_summed = sem("mod_summed")
        mod_used = sem("mod_used")
        late_loaded = sem("late_loaded")
        toep_loaded = [sem("toep_loaded0"), sem("toep_loaded1")]
        ctx_ss_ready = sem("ctx_ss_ready")
        ctx_ms_ready = sem("ctx_ms_ready")
        ctx_rt_ready = sem("ctx_rt_ready")
        hc_scaled = sem("hc_scaled")
        hc_high = sem("hc_high")
        hc_ready = sem("hc_ready")
        kc_mm = sem("kc_mm")
        kc_read = sem("kc_read")
        sq_ready = sem("sq_ready")
        hn_ready = sem("hn_ready")
        hn_root = sem("hn_root")
        item_ready = sem("item_ready")
        vt_ready = sem("vt_ready")
        v_mm = sem("v_mm")
        v_ready = sem("v_ready")
        bias_ready = sem("bias_ready")
        s_ready = sem("s_ready")
        min_ready = sem("min_ready")
        exp_ready = sem("exp_ready")
        prob_ready = sem("prob_ready")
        turned = sem("turned")
        pt_ready = sem("pt_ready")
        o_ready = sem("o_ready")
        o_split = sem("o_split")
        conv_ready = sem("conv_ready")
        out_stored = sem("out_stored")

        by_group = mod[:, :].rearrange("p (g s w) -> p g s w", s=MOD_GROUP, w=2)

        def vector(which, m=0, who=0):
            if who:
                return mod_ctx[:, (which * DT + m) * 2:(which * DT + m) * 2 + 1]
            at_tile = MOD_ORDER.index(which * DT + m)
            return mod[:, at_tile * 2:at_tile * 2 + 1]

        def all_of(which, who=0):
            if who:
                return mod_ctx[:, 2 * which * DT:2 * (which + 1) * DT].rearrange(
                    "p (g s w) -> p g s w", s=MOD_CTX, w=2)[:, :, :, 0]
            if which < 2:
                g = which * DT // MOD_CTX
                return by_group[:, g:g + DT // MOD_CTX, 0:MOD_CTX, 0]
            g = (which - 2) * DT // MOD_REST
            return by_group[:, g:g + DT // MOD_REST, MOD_CTX:, 0]

        block = ctx.enter_context(nc.Block())

        @block.sync
        def _(sp):
            for j in range(X_PARTS):
                part = slice(j * X_PART, (j + 1) * X_PART)
                sp.dma_start(X[:, part, :], x[:, part, :]).then_inc(x_loaded[j], 16)
            for q in range(RING):
                sp.dma_start(w_raw[:, q, :], weights[q]).then_inc(w_loaded[q], 16)

            def load_rounds(first, last):
                with sp.Fori(first, last) as i:
                    for q in range(RING):
                        sp.wait_ge(w_lo_ready, i * RING + (q - RING + 1))
                        sp.dma_start(w_raw[:, q, :], weights[i * RING + q]).then_inc(w_loaded[q], 16)

            load_rounds(1, ATT_ROUND)
            sp.wait_ge(jobs_done, ATT_JOB - FF_GROUP_JOBS + RING)
            sp.dma_start(ctx_sb[:, :, :], ctx_in).then_inc(ctx_loaded, 16)
            load_rounds(ATT_ROUND, ROUNDS)

            for m in range(DT):
                sp.wait_ge(bank_free, ROUNDS * RING - DT + RING + m + 1)
                sp.dma_start(out[:, m, :], X[:, m, :]).then_inc(out_stored, 16)
            sp.wait_ge(out_stored, 16 * DT)

        @block.gpsimd
        def _(pool):
            def low(n, q):
                pool.wait_ge(w_hi_ready, n + 1)
                nc.gpsimd.tensor_tensor(w_lo[:, q, :], w_raw[:, q, :], w_hi[:, q, :].bitcast(F32),
                                        ALU.subtract).then_inc(w_lo_ready, 1)

            def low_rounds(first, last):
                with pool.Fori(first, last) as i:
                    for q in range(RING):
                        low(i * RING + q, q)

            low_rounds(0, ATT_ROUND)
            with pool.Fori(0, QUARTERS // 2) as b:
                for half in range(2):
                    for s in range(QT_JOBS):
                        low(b * (2 * QT_JOBS) + (ATT_JOB + half * QT_JOBS + s), (half * QT_JOBS + s) % RING)
                    pool.wait_ge(late_loaded, 16 * LATE)
                    for hh in range(QT_HEADS):
                        head = b * (2 * QT_HEADS) + (half * QT_HEADS + hh)
                        side = hh % 2
                        pool.wait_ge(toep_loaded[side], (b * QT_HEADS + (half * QT_HEADS + hh) // 2 + 1) * 16)
                        pool.wait_ge(min_ready, head * TOK + TOK)
                        for kind in range(3):
                            n = REAL_KEYS[kind]
                            o = kind * UNIT_KEYS + REAL[kind].start
                            t = TOEPLITZ_OFF[kind]
                            last = nc.gpsimd.tensor_tensor(
                                bias[:, side, o:o + n], mask_sb[:, MASK_OFF[kind]:MASK_OFF[kind] + n],
                                toeplitz[:, side, t:t + n], ALU.subtract)
                        last.then_inc(bias_ready, 1)
            low_rounds(WO_ROUND, ROUNDS)

        @block.tensor
        def _(pe):
            def product(dst, w, xs, start, stop):
                for a, (l, r) in enumerate(((0, 0), (0, 1), (1, 0))):
                    mm = nc.tensor.matmul(dst, w[l], xs[r], start=start and a == 0, stop=stop and a == 2)
                return mm

            def job(n, q, hi, lo, tiles, kt=DT):
                pe.wait_ge(w_lo_ready, n + 1)
                pe.wait_ge(bank_free, n + 1)
                for k in range(kt):
                    if tiles is not None:
                        pe.wait_ge(tiles_ready, tiles + (k + 1))
                    mm = product(ps[:, q, :], (w_hi[:, q, k * P:(k + 1) * P], w_lo[:, q, k * P:(k + 1) * P]),
                                 (hi[:, k, :], lo[:, k, :]), k == 0, k == kt - 1)
                mm.then_inc(jobs_done, 1)

            def jobs(n0, count, hi, lo, tiles, kt=DT, before=None):
                with pe.Fori(0, count // RING) as i:
                    for q in range(RING):
                        if before is not None and q == 0:
                            pe.wait_ge(*before)
                        job(n0 + i * RING + q, q, hi, lo, tiles, kt)

            def norm_sum(v):
                pe.wait_ge(ss_ready, v + 1)
                nc.tensor.matmul(ps[:, NORM_BANK, :], ones[:, :], E[:, SUMSQ, :], start=True,
                                 stop=True).then_inc(ms_ready, 1)

            def value_jobs(n0, tiles):
                pe.wait_ge(bank_free, n0 + RING)
                for i in range(V_JOBS // RING):
                    for q in range(RING):
                        pe.wait_ge(w_lo_ready, n0 + i * RING + (q + 1))
                        for kk in range(V_TILES):
                            k = q * V_TILES + kk
                            pe.wait_ge(tiles_ready, tiles + (k + 1))
                            for t in range(TOK):
                                mm = product(ps[:, i * TOK + t, :],
                                             (H_hi[:, k, t * P:(t + 1) * P], H_lo[:, k, t * P:(t + 1) * P]),
                                             [w[:, q, kk * V_WIDE:(kk + 1) * V_WIDE] for w in (w_hi, w_lo)],
                                             k == 0, k == DT - 1)
                        mm.then_inc(jobs_done, 1)

            def attention(L):
                pe.wait_ge(tiles_ready, L * LAYER_TILES + TILE_OG)

                def scores(u):
                    h, j = divmod(u, TOK)
                    if u >= 3:
                        pe.wait_ge(st_ready, L * (RH * TOK) + (u - 2))
                    k_tile = slice(j * P, (j + 1) * P)
                    product(ps[:, RET_BANKS[u % 3], 0:S - j * P], (A_hi[:, RH + h, k_tile], A_lo[:, RH + h, k_tile]),
                            (A_hi[:, h, j * P:S], A_lo[:, h, j * P:S]), True, True).then_inc(sc_ready, 1)

                def values(u):
                    h, j = divmod(u, TOK)
                    pe.wait_ge(st_ready, L * (RH * TOK) + (u + 1))
                    if j == 0 and h >= 2:
                        pe.wait_ge(o_copied, L * RH + (h - 1))
                    n = S - j * P
                    for t in range(2):
                        v = slice((2 * h + t) * P, (2 * h + t + 1) * P)
                        mm = product(ps[:, O_BANKS[h % 2] + t, j * P:S], (V_hi[:, j, v], V_lo[:, j, v]),
                                     (ST[:, u % 3, 0, 0:n], ST[:, u % 3, 1, 0:n]), j == 0, j == TOK - 1)
                    mm.then_inc(pv_done, 1)

                def variance(h):
                    pe.wait_ge(o_copied, L * RH + (h + 1))
                    if h:
                        pe.wait_ge(dev_ready, L * RH + h)
                    nc.tensor.matmul(ps[:, VAR_BANK, :], ones[:, :], Alf[:, h, :], start=True, stop=False)
                    nc.tensor.matmul(ps[:, VAR_BANK, :], ones[:, :], Alf[:, RH + h, :], start=False,
                                     stop=True).then_inc(var_ready, 1)

                units = RH * TOK
                scores(0)
                scores(1)
                for u in range(units):
                    if u + 2 < units:
                        scores(u + 2)
                    values(u)
                    if u % TOK == 1 and u > TOK:
                        variance(u // TOK - 1)
                variance(RH - 1)

            pe.sem_inc(jobs_done, RING)
            pe.sem_inc(bank_free, RING)
            pe.sem_inc(mod_used, 1)

            with pe.Fori(0, DEPTH) as L:
                n = L * LAYER_JOBS
                tiles = L * LAYER_TILES
                norm_sum(2 * L)
                value_jobs(n + JOB_V, tiles + TILE_H)
                jobs(n + JOB_QK, QK_JOBS, H_hi, H_lo, tiles + TILE_H)
                attention(L)
                jobs(n + JOB_G, G_JOBS, H_hi, H_lo, tiles + TILE_H, before=(dev_ready, L * RH + RH))
                with pe.Fori(0, PAIR_JOBS // RING) as i:
                    for q in range(RING):
                        if q % 2 == 0:
                            job(n + JOB_RET + i * RING + q, q, H_hi, H_lo, tiles + TILE_H)
                        else:
                            job(n + JOB_RET + i * RING + q, q, C_hi, C_lo, tiles + TILE_OG)
                jobs(n + JOB_CONV, CONV_JOBS, H_hi, H_lo, tiles + TILE_H)
                with pe.Fori(0, PAIR_JOBS // RING) as i:
                    for q in range(RING):
                        if q % 2 == 0:
                            job(n + JOB_MIX + i * RING + q, q, H_hi, H_lo, tiles + TILE_H)
                        else:
                            job(n + JOB_MIX + i * RING + q, q, B_hi, B_lo, tiles + TILE_BZ)
                jobs(n + JOB_O, O_JOBS, A_hi, A_lo, tiles + TILE_MIX)
                norm_sum(2 * L + 1)
                with pe.Fori(0, FF_GROUPS // 2) as g2:
                    for half, (hi, lo) in enumerate(((A_hi, A_lo), (C_hi, C_lo))):
                        g = g2 * 2 + half
                        ng = n + JOB_FF + g2 * (2 * FF_GROUP_JOBS) + half * FF_GROUP_JOBS
                        jobs(ng, DT, H_hi, H_lo, tiles + TILE_H2)
                        jobs(ng + DT, DT, hi, lo, tiles + TILE_FF + g2 * (2 * DT) + half * DT)
                        pe.wait_ge(mod_summed, L * FF_GROUPS + g + 1)
                        for s in range(MOD_GROUP):
                            nc.tensor.matmul(ps[:, MOD_BANK, bass.ds((g * MOD_GROUP + s) * 2, 2)], mod_w[:, s, 0:P],
                                             ones[:, 0:2], start=True, stop=True)
                        for s in range(MOD_CTX):
                            mm = nc.tensor.matmul(ps[:, MOD_BANK, bass.ds((g * MOD_CTX + s + MOD_LAYER) * 2, 2)],
                                                  ctx_acc[:, s, :], ones[:, 0:2], start=True, stop=True)
                        mm.then_inc(mod_used, 1)

            norm_sum(2 * DEPTH)
            norm_sum(2 * DEPTH + 1)
            pe.wait_ge(ctx_ss_ready, 1)
            nc.tensor.matmul(ps[:, MOD_BANK, 0:CTX], ones[:, :], ctx_sum[:, :], start=True,
                             stop=True).then_inc(ctx_ms_ready, 1)

            pe.wait_ge(late_loaded, 16 * LATE)

            def quarter(b, half):
                n0 = b * (2 * QT_JOBS) + (ATT_JOB + half * QT_JOBS)
                item0 = b * (2 * ITEMS) + half * ITEMS

                def slot(s):
                    return (half * QT_JOBS + s) % RING

                def head_sums(i):
                    width = CTX if i in (2, 4) else S
                    pe.wait_ge(sq_ready, item0 + (i + 1))
                    if i >= 2:
                        pe.wait_ge(hn_root, item0 + (i - 1))
                    nc.tensor.matmul(ps[:, 4 + i % 2, 0:width], block_sb[:, :], prob[:, i % 2, 0:width],
                                     start=True, stop=True).then_inc(hn_ready, 1)

                def ctx_product(s, t, col):
                    q = slot(s)
                    pe.wait_ge(w_lo_ready, n0 + (s + 1))
                    for k in range(DT):
                        pe.wait_ge(hc_ready, k + 1)
                        mm = product(ps[:, 6 + t, col:col + CTX],
                                     (w_hi[:, q, k * P:(k + 1) * P], w_lo[:, q, k * P:(k + 1) * P]),
                                     (HC_hi[:, k, :], HC_lo[:, k, :]), k == 0, k == DT - 1)
                    return mm

                def ctx_keys(s, t):
                    ctx_product(s, t, 0).then_inc(kc_mm, 1)

                def turn_values():
                    pe.wait_ge(vt_ready, (b * 2 + half) * QT_TILES + QT_TILES)
                    for tile in range(7):
                        for t in range(QT_TILES):
                            if tile < len(V_STARTS):
                                src = vt[:, t, V_STARTS[tile]:V_STARTS[tile] + P]
                            else:
                                src = vt_ctx[:, t, (tile - 5) * P:(tile - 4) * P]
                            c = (tile % 2) * V_COLS + t * P
                            mm = nc.tensor.transpose(ps[:, 4 + tile // 2, c:c + P], src, ident_sb[:, :])
                        if tile % 2 or tile == 6:
                            mm.then_inc(v_mm, 1)

                tiles = ATT_TILE
                job(n0, slot(0), H_hi, H_lo, tiles)
                job(n0 + 1, slot(1), H_hi, H_lo, tiles)
                head_sums(0)
                ctx_keys(2, 0)
                head_sums(1)
                job(n0 + 2, slot(2), H_hi, H_lo, tiles)
                head_sums(2)
                ctx_keys(3, 1)
                head_sums(3)
                job(n0 + 3, slot(3), H_hi, H_lo, tiles)
                head_sums(4)
                pe.wait_ge(kc_read, (b * 2 + half) * QT_TILES + 1)
                ctx_product(4, 0, CTX)
                head_sums(5)
                job(n0 + 4, slot(4), H_hi, H_lo, tiles)
                pe.wait_ge(kc_read, (b * 2 + half) * QT_TILES + 2)
                ctx_product(5, 1, CTX)
                job(n0 + 5, slot(5), H_hi, H_lo, tiles)
                pe.wait_ge(hn_root, item0 + ITEMS)
                turn_values()

                unit0 = (b * 2 + half) * QT_UNITS
                head0 = (b * 2 + half) * QT_HEADS
                pe.wait_ge(item_ready, item0 + ITEMS)

                def scores(u):
                    hh, i = divmod(u, TOK)
                    t, rows = hh // 2, slice(HD * (hh % 2), HD * (hh % 2) + HD)
                    qs = (q_hi[rows, t, i * P:(i + 1) * P], q_lo[rows, t, i * P:(i + 1) * P])
                    step = S - KEY0[i]
                    first = t * (S + CTX) + KEY0[i]
                    ks = [x[rows, first:first + 2 * step].rearrange("p (a n) -> p a n", n=step)[:, :, 0:KEYS]
                          for x in (k_hi, k_lo)]
                    product(ps[:, SCORE_BANKS[u % 3], :], qs, ks, True, True).then_inc(s_ready, 1)

                def turn(u):
                    pe.wait_ge(prob_ready, unit0 + (u + 1))
                    for c, at_col in enumerate(CHUNK_COLS[u % TOK]):
                        mm = nc.tensor.transpose(ps[:, TURN_BANKS[u % 3], c * P:(c + 1) * P],
                                                 prob[:, u % 3, at_col:at_col + P], ident_sb[:, :])
                    mm.then_inc(turned, 1)

                def weigh(pair_):
                    hh, side = divmod(pair_, TOK // 2)
                    cols = slice((hh // 2) * P, (hh // 2 + 1) * P)
                    pe.wait_ge(pt_ready, unit0 + 2 * pair_ + 2)
                    if side == 0 and hh >= 2:
                        pe.wait_ge(o_split, head0 + (hh - 1))
                    o0 = side * 2 * P
                    buf = pair_ % 2
                    for c, tile in enumerate((VX0, VX1, SHARED_V[side])):
                        nc.tensor.matmul(ps[:, 2 + hh % 2, o0:o0 + 2 * P], v_sb[:, tile, cols],
                                         pt[:, buf, c, :, :].rearrange("p t n -> p (t n)"), start=c == 0, stop=False)
                    for t, (tile, rows) in enumerate(OWN_V[side]):
                        mm = nc.tensor.matmul(ps[:, 2 + hh % 2, o0 + t * P:o0 + (t + 1) * P], v_sb[rows, tile, cols],
                                              pt[rows, buf, 3, t, :], start=False, stop=t == 1)
                    if side == TOK // 2 - 1:
                        mm.then_inc(o_ready, 1)

                pe.wait_ge(v_ready, (b * 2 + half) * 4 + 1)
                scores(0)
                pe.wait_ge(v_ready, (b * 2 + half) * 4 + 2)
                scores(1)
                pe.wait_ge(v_ready, (b * 2 + half) * 4 + 4)
                for u in range(QT_UNITS):
                    if u + 2 < QT_UNITS:
                        scores(u + 2)
                    if u >= 3 and u % 2:
                        weigh((u - 3) // 2)
                    turn(u)
                weigh(QT_UNITS // 2 - 1)
                pe.wait_ge(o_split, head0 + QT_HEADS)

            with pe.Fori(0, QUARTERS // 2) as b:
                for half in range(2):
                    quarter(b, half)
            jobs(WO_ROUND * RING, DT, A_hi, A_lo, None)
            norm_sum(2 * DEPTH + 2)
            n, tile = FF2_ROUND * RING, ATT_TILE + 2 * DT
            for g, kt in enumerate(FF2_GROUPS):
                hi, lo = ((A_hi, A_lo), (B_hi, B_lo))[g % 2]
                jobs(n, 2 * kt, H_hi, H_lo, ATT_TILE + DT)
                jobs(n + 2 * kt, DT, hi, lo, tile, kt)
                n += 2 * kt + DT
                tile += kt


        @block.scalar
        def _(act):
            act.dma_start(par[:, :], params).then_inc(par_loaded, 16)
            act.dma_start(z_pos[:, :], positions).then_inc(par_loaded, 16)

            def ahead(r, q):
                s = (q + RING - 1) % RING
                m = r if q == 0 else r + 1
                if isinstance(m, int) and m >= ROUNDS:
                    return
                act.wait_ge(w_loaded[s], (m + 1) * 16)
                act.wait_ge(jobs_done, m * RING + (s + 1))
                nc.scalar.activation(w_hi[:, s, :], w_raw[:, s, :], ACT.Copy).then_inc(w_hi_ready, 1)

            def phase(r0, rounds, epilogue=None, per_body=1):
                with act.Fori(0, rounds // per_body) as i:
                    for s in range(per_body * RING):
                        r, q = r0 + i * per_body + s // RING, s % RING
                        ahead(r, q)
                        if epilogue is not None:
                            epilogue(r, i, s)

            def evacuate(r, q, func, dst):
                act.wait_ge(jobs_done, r * RING + (q + 1 + RING))
                nc.scalar.activation(dst, ps[:, q, :], func).then_inc(ev_ready, 1)

            def gates(dst):
                def epilogue(r, i, s):
                    if s % 2 == 0:
                        evacuate(r, s, ACT.Sigmoid, dst[:, s, :])
                return epilogue

            def root(v):
                act.wait_ge(ms_ready, v + 1)
                nc.scalar.activation(E[:, ROOT, :], ps[:, NORM_BANK, :], ACT.Sqrt, bias=eps[:, :],
                                     scale=1.0 / D).then_inc(rt_ready, 1)

            def first_high(q):
                act.wait_ge(w_loaded[q], 16)
                nc.scalar.activation(w_hi[:, q, :], w_raw[:, q, :], ACT.Copy).then_inc(w_hi_ready, 1)

            def high_parts(v, shift=None):
                for m in range(DT):
                    act.wait_ge(h_scaled, v * DT + (m + 1))
                    if shift is None:
                        high = nc.scalar.activation(H_hi[:, m, :], Hlf[:, m, :], ACT.Copy)
                    else:
                        high = nc.scalar.activation(H_hi[:, m, :], Hlf[:, m, :], ACT.Identity, bias=vector(shift, m))
                    high.then_inc(h_high, 1)

            act.wait_ge(par_loaded, 32)
            nc.scalar.activation(cond[:, :, :], par[:, PAR_COND:PAR_COND + 2 * DT], ACT.Sigmoid).then_inc(cond_sig, 1)
            for j in range(X_PARTS):
                part = slice(j * X_PART, (j + 1) * X_PART)
                act.wait_ge(x_loaded[j], 16)
                nc.scalar.activation(Hf[:, part, :], X[:, part, :], ACT.Square).then_inc(x_squared, 1)
            act.dma_start(decay_sb[:, :, :], decay).then_inc(decay_loaded, 16)
            act.wait_ge(angles_ready, 1)
            nc.scalar.activation(rope[:, 0, :], Cf[:, 4, :], ACT.Sin).then_inc(sines_ready, 1)
            nc.scalar.activation(rope[:, 1, :], Cf[:, 5, :], ACT.Sin).then_inc(sines_ready, 1)
            first_high(0)
            root(0)
            for q in range(1, RING - 1):
                first_high(q)

            with act.Fori(0, DEPTH) as L:
                r = L * (LAYER_JOBS // RING)
                high_parts(2 * L)
                phase(r + JOB_V // RING, (V_JOBS + QK_JOBS) // RING)
                for h in range(RH):
                    act.wait_ge(pv_done, L * (RH * TOK) + TOK * (h + 1))
                    for t in range(2):
                        nc.scalar.activation(Clf[:, 2 * h + t, :], ps[:, O_BANKS[h % 2] + t, :], ACT.Copy)
                        sq = nc.scalar.activation(Alf[:, h + RH * t, :], ps[:, O_BANKS[h % 2] + t, :], ACT.Square)
                    sq.then_inc(o_copied, 1)
                    act.wait_ge(var_ready, L * RH + (h + 1))
                    nc.scalar.activation(Af[:, h, :], ps[:, VAR_BANK, :], ACT.Sqrt, bias=eps[:, :],
                                         scale=1.0 / RV).then_inc(dev_ready, 1)
                phase(r + JOB_G // RING, G_JOBS // RING,
                      lambda r, i, s: evacuate(r, s, ACT.Sigmoid, Bf[:, s, :]))
                phase(r + JOB_RET // RING, PAIR_JOBS // RING, gates(Bf))

                def conv_in(r, i, s):
                    if s % 3 == 0:
                        evacuate(r, s % RING, ACT.Copy, Cf[:, s % RING, :])
                phase(r + JOB_CONV // RING, CONV_JOBS // RING, conv_in, per_body=3)
                phase(r + JOB_MIX // RING, PAIR_JOBS // RING, gates(Cf))
                phase(r + JOB_O // RING, O_JOBS // RING)
                root(2 * L + 1)
                high_parts(2 * L + 1)
                with act.Fori(0, FF_GROUPS) as g:
                    rg = r + JOB_FF // RING + g * (FF_GROUP_JOBS // RING)
                    act.wait_ge(mod_used, L * FF_GROUPS + g + 1)
                    act.dma_start(mod_w[:, :, :], mod_weights[L * FF_GROUPS + g]).then_inc(mod_loaded, 16)
                    phase(rg, DT // RING, lambda r, i, s: evacuate(r, s, ACT.Relu, E[:, s, :]))
                    phase(rg + DT // RING, DT // RING)
                root(2 * L + 2)

            act.wait_ge(ctx_loaded, 16)
            nc.scalar.activation(ctx_sq[:, :, :], ctx_sb[:, :, :], ACT.Square).then_inc(ctx_squared, 1)
            act.wait_ge(jobs_done, ATT_JOB + RING)
            act.wait_ge(mod_used, DEPTH * FF_GROUPS + 1)
            act.dma_start(mask_sb[:, :], key_mask).then_inc(late_loaded, 16)
            act.dma_start(block_sb[:, :], block_ones).then_inc(late_loaded, 16)
            act.dma_start(ident_sb[:, :], ident).then_inc(late_loaded, 16)
            for side in range(2):
                act.dma_start(toeplitz[:, side, :], rpb[side]).then_inc(toep_loaded[side], 16)
            for m in range(DT):
                act.wait_ge(xn_ready, m + 1)
                nc.scalar.activation(Hf[:, m, :], X[:, m, :], ACT.Square).then_inc(xn_squared, 1)
            root(2 * DEPTH + 1)
            act.wait_ge(ctx_ms_ready, 1)
            nc.scalar.activation(ctx_root[:, :], ps[:, MOD_BANK, 0:CTX], ACT.Sqrt, bias=eps[:, :],
                                 scale=1.0 / D).then_inc(ctx_rt_ready, 1)
            high_parts(2 * DEPTH, SH1)
            for m in range(DT):
                act.wait_ge(hc_scaled, m + 1)
                nc.scalar.activation(HC_hi[:, m, :], HC_lo_f[:, m, :], ACT.Identity,
                                     bias=vector(SH1, m, 1)).then_inc(hc_high, 1)

            def quarter(b, half):
                r0 = b * (2 * QT_JOBS // RING) + ATT_ROUND
                item0 = b * (2 * ITEMS) + half * ITEMS
                unit0 = (b * 2 + half) * QT_UNITS

                def place(s):
                    n = half * QT_JOBS + s
                    return r0 + n // RING, n % RING

                def squares(i):
                    s, is_ctx = ((0, False), (1, False), (2, True), (2, False), (3, True), (3, False))[i]
                    if is_ctx:
                        t = s - 2
                        act.wait_ge(kc_mm, (b * 2 + half) * QT_TILES + (t + 1))
                        src, width = ps[:, 6 + t, 0:CTX], CTX
                    else:
                        r, q = place(s)
                        act.wait_ge(jobs_done, r * RING + (q + 1 + RING))
                        src, width = ps[:, q, :], S
                    if i >= 2:
                        act.wait_ge(hn_ready, item0 + (i - 1))
                    nc.scalar.activation(prob[:, i % 2, 0:width], src, ACT.Square).then_inc(sq_ready, 1)

                def head_roots(i):
                    width = CTX if i in (2, 4) else S
                    act.wait_ge(hn_ready, item0 + (i + 1))
                    if i >= 2:
                        act.wait_ge(item_ready, item0 + (i - 1))
                    nc.scalar.activation(head_root[:, i % 2, 0:width], ps[:, 4 + i % 2, 0:width], ACT.Sqrt,
                                         bias=eps[:, :], scale=1.0 / HD).then_inc(hn_root, 1)

                def exponentials(u):
                    s = u % 3
                    act.wait_ge(min_ready, unit0 + (u + 1 + 2 * TOK))
                    nc.scalar.activation(prob[:, s, :], prob[:, s, :], ACT.Exp,
                                         bias=stat[:, MIN + s:MIN + s + 1], scale=-1.0,
                                         accum_out=stat[:, SUM + s:SUM + s + 1]).then_inc(exp_ready, 1)

                def copy_turned(u):
                    act.wait_ge(turned, unit0 + (u + 1))
                    nc.scalar.activation(pt[:, (u // 2) % 2, :, u % 2, :],
                                         ps[:, TURN_BANKS[u % 3], :].rearrange("p (c n) -> p c n", n=P),
                                         ACT.Copy).then_inc(pt_ready, 1)

                ahead(*place(0))
                squares(0)
                ahead(*place(1))
                squares(1)
                head_roots(0)
                squares(2)
                head_roots(1)
                ahead(*place(2))
                squares(3)
                head_roots(2)
                squares(4)
                head_roots(3)
                squares(5)
                head_roots(4)
                head_roots(5)
                for s in (3, 4, 5):
                    ahead(*place(s))
                exponentials(0)
                exponentials(1)
                for u in range(QT_UNITS):
                    if u + 2 < QT_UNITS:
                        exponentials(u + 2)
                    copy_turned(u)
                    if u % TOK == TOK - 1:
                        head = b * (2 * QT_HEADS) + (half * QT_HEADS + u // TOK)
                        side = (u // TOK) % 2
                        act.wait_ge(bias_ready, head + 1)
                        act.dma_start(toeplitz[:, side, :], rpb[head + 2]).then_inc(toep_loaded[side], 16)

            with act.Fori(0, QUARTERS // 2) as b:
                for half in range(2):
                    quarter(b, half)
            phase(WO_ROUND, DT // RING)
            root(2 * DEPTH + 2)
            high_parts(2 * DEPTH + 1, SH2)
            r, m0 = FF2_ROUND, 0
            for g, kt in enumerate(FF2_GROUPS):
                def gate(r, i, s):
                    if s % 2:
                        return
                    t = s // 2
                    act.wait_ge(jobs_done, r * RING + (s + 1 + RING))
                    nc.scalar.activation(gated[:, t, 1:S + 1], ps[:, s, :], ACT.Copy).then_inc(ev_ready, 1)
                    m = i * 2 + (m0 + t)
                    act.wait_ge(conv_ready, m + 1)
                    nc.scalar.activation(conv[:, t, :], conv[:, t, :], ACT.Gelu,
                                         bias=par[:, bass.ds(m + PAR_CB2, 1)]).then_inc(ev_ready, 1)
                phase(r, 2 * kt // RING, gate)
                if g < len(FF2_GROUPS) - 1:
                    phase(r + 2 * kt // RING, DT // RING)
                else:
                    for k in range(DT):
                        ahead(ROUNDS - DT // RING + k // RING, k % RING)
                r += (2 * kt + DT) // RING
                m0 += kt
            act.wait_ge(toep_loaded[0], 16 * (NH // 2 + 1))
            act.wait_ge(toep_loaded[1], 16 * (NH // 2 + 1))


        @block.vector
        def _(dve):
            fence = dve.drain
            V = nc.vector

            def split(whole, hi, lo, ready=tiles_ready):
                fence()
                V.tensor_copy(hi, whole)
                fence()
                V.tensor_tensor(lo, whole, hi.bitcast(F32), ALU.subtract).then_inc(ready, 1)

            def column(base, L, m=0):
                return par[:, bass.ds(L * PAR_LAYER + m + base, 1)]

            def job_done(r, q):
                dve.wait_ge(jobs_done, r * RING + (q + 1 + RING))

            def sum_squares(m, first):
                fence()
                V.tensor_tensor(E[:, 0, :], X[:, m, :], X[:, m, :], ALU.mult)
                fence()
                if first:
                    return V.tensor_copy(E[:, SUMSQ, :], E[:, 0, :])
                return V.tensor_tensor(E[:, SUMSQ, :], E[:, SUMSQ, :], E[:, 0, :], ALU.add)

            def norm(v, gain):
                dve.wait_ge(rt_ready, v + 1)
                V.reciprocal(E[:, ROOT, :], E[:, ROOT, :])
                fence()
                def scaled(m):
                    V.scalar_tensor_tensor(out=Hlf[:, m, :], in0=X[:, m, :], scalar=gain(m),
                                           in1=E[:, ROOT, :], op0=ALU.mult, op1=ALU.mult).then_inc(h_scaled, 1)

                def low(m):
                    dve.wait_ge(h_high, v * DT + (m + 1))
                    V.tensor_tensor(H_lo[:, m, :], Hlf[:, m, :], H_hi[:, m, :].bitcast(F32),
                                    ALU.subtract).then_inc(tiles_ready, 1)

                scaled(0)
                for m in range(DT):
                    if m + 1 < DT:
                        scaled(m + 1)
                    low(m)

            def add_to_stream(r, i, q, squares=False, first=False):
                job_done(r, q)
                m = i * RING + q
                add = V.tensor_tensor(X[:, m, :], X[:, m, :], ps[:, q, :], ALU.add)
                add.then_inc(bank_free, 1)
                if squares:
                    return sum_squares(m, first)

            V.memset(ones[:, :], 1.0)
            V.memset(eps[:, :], EPS)

            def add_square(m):
                fence()
                if m == 0:
                    return V.tensor_copy(E[:, SUMSQ, :], Hf[:, 0, :])
                return V.tensor_tensor(E[:, SUMSQ, :], E[:, SUMSQ, :], Hf[:, m, :], ALU.add)

            dve.wait_ge(par_loaded, 32)
            V.tensor_copy(Cf[:, 0, :], z_pos[:, :])
            fence()
            V.tensor_scalar(Cf[:, 0, :], Cf[:, 0, :], par[:, PAR_FREQ:PAR_FREQ + 1], None, ALU.mult)
            for which, shift in ((0, 0.25), (1, 0.0)):
                fence()
                V.tensor_scalar(Cf[:, 1, :], Cf[:, 0, :], INV_2PI, shift, ALU.mult, ALU.add)
                fence()
                V.tensor_scalar(Cf[:, 1, :], Cf[:, 1, :], ROUND_MAGIC, None, ALU.add)
                fence()
                V.tensor_scalar(Cf[:, 1, :], Cf[:, 1, :], -ROUND_MAGIC, None, ALU.add)
                fence()
                V.scalar_tensor_tensor(out=Cf[:, 2, :], in0=Cf[:, 1, :], scalar=-TWO_PI_1, in1=Cf[:, 0, :],
                                       op0=ALU.mult, op1=ALU.add)
                fence()
                V.scalar_tensor_tensor(out=Cf[:, 3, :], in0=Cf[:, 1, :], scalar=-TWO_PI_2, in1=Cf[:, 2, :],
                                       op0=ALU.mult, op1=ALU.add)
                fence()
                V.scalar_tensor_tensor(out=Cf[:, 2, :], in0=Cf[:, 1, :], scalar=-TWO_PI_3, in1=Cf[:, 3, :],
                                       op0=ALU.mult, op1=ALU.add)
                fence()
                if which == 0:
                    V.tensor_scalar(Cf[:, 2, :], Cf[:, 2, :], HALF_PI, None, ALU.add)
                    fence()
                V.tensor_scalar(Cf[:, 4 + which, :], Cf[:, 2, :], PI_LOW, -PI_LOW, ALU.min, ALU.max)
            fence()
            V.tensor_scalar(Cf[P // 2:P, 5, :], Cf[P // 2:P, 5, :], -1.0, None, ALU.mult).then_inc(angles_ready, 1)
            dve.wait_ge(cond_sig, 1)
            V.tensor_tensor(cond[:, :, :].rearrange("p k c -> p (k c)"), cond[:, :, :].rearrange("p k c -> p (k c)"),
                            par[:, PAR_COND:PAR_COND + 2 * DT], ALU.mult)
            for m in range(DT):
                if m % X_PART == 0:
                    dve.wait_ge(x_squared, m // X_PART + 1)
                last = add_square(m)
            last.then_inc(ss_ready, 1)

            with dve.Fori(0, DEPTH) as L:
                r = L * (LAYER_JOBS // RING)
                norm(2 * L, lambda m: column(PAR_NORM1 + m, L))

                for i in range(V_JOBS // RING):
                    job_done(r + (JOB_V // RING + i), RING - 1)
                    for t in range(TOK):
                        bank = ps[:, i * TOK + t, :].rearrange("p (h v) -> p h v", v=RV)
                        V.tensor_reduce(small[:, 0:2], bank, AX_X, ALU.add)
                        fence()
                        V.tensor_scalar(small[:, 2:4], small[:, 0:2], -1.0 / RV, None, ALU.mult)
                        fence()
                        for h in range(2):
                            last = V.tensor_scalar(Cf[:, 0, h * RV:(h + 1) * RV], bank[:, h, :],
                                                   small[:, 2 + h:3 + h], None, ALU.add)
                        if i == 0:
                            last.then_inc(bank_free, 2)
                        cols = slice(i * 512, (i + 1) * 512)
                        split(Cf[:, 0, :], V_hi[:, t, cols], V_lo[:, t, cols])

                fence()
                dve.wait_ge(sines_ready, 2)
                dve.wait_ge(decay_loaded, 16)
                with dve.Fori(0, QK_JOBS // RING) as i:
                    for q in range(RING):
                        job_done(r + JOB_QK // RING + i, q)
                        half = P // 2
                        V.tensor_tensor(Cf[:, 0, :], ps[:, q, :], rope[:, 0, :], ALU.mult)
                        V.tensor_tensor(Cf[half:P, 1, :], ps[0:half, q, :], rope[0:half, 1, :], ALU.mult)
                        V.tensor_tensor(Cf[0:half, 1, :], ps[half:P, q, :], rope[half:P, 1, :],
                                        ALU.mult).then_inc(bank_free, 1)
                        fence()
                        m = i * RING + q
                        V.tensor_tensor(Alf[:, m, :], Cf[:, 0, :], Cf[:, 1, :], ALU.add)
                        split(Alf[:, m, :], A_hi[:, m, :], A_lo[:, m, :])

                for u in range(RH * TOK):
                    h, j = divmod(u, TOK)
                    n = S - j * P
                    dve.wait_ge(sc_ready, L * (RH * TOK) + (u + 1))
                    if u >= 3:
                        dve.wait_ge(pv_done, L * (RH * TOK) + (u - 2))
                    V.tensor_tensor(st_tmp[:, u % 2, 0:n], ps[:, RET_BANKS[u % 3], 0:n], decay_sb[:, h, 0:n], ALU.mult)
                    split(st_tmp[:, u % 2, 0:n], ST[:, u % 3, 0, 0:n], ST[:, u % 3, 1, 0:n], st_ready)

                for i in range(G_JOBS // RING):
                    for q in range(RING):
                        m = i * RING + q
                        if m % 2 == 0:
                            dve.wait_ge(dev_ready, L * RH + (m // 2 + 1))
                            V.reciprocal(Af[:, m // 2, :], Af[:, m // 2, :])
                        fence()
                        dve.wait_ge(ev_ready, L * EV_LAYER + (EV_G + m + 1))
                        V.tensor_tensor(Bf[:, 4, :], Bf[:, q, :], ps[:, q, :], ALU.mult).then_inc(bank_free, 1)
                        V.scalar_tensor_tensor(out=Bf[:, 5, :], in0=Clf[:, m, :], scalar=column(PAR_RET + m, L),
                                               in1=Af[:, m // 2, :], op0=ALU.mult, op1=ALU.mult)
                        fence()
                        V.tensor_tensor(Clf[:, m, :], Bf[:, 4, :], Bf[:, 5, :], ALU.mult)
                        split(Clf[:, m, :], C_hi[:, m, :], C_lo[:, m, :])

                with dve.Fori(0, PAIR_JOBS // RING) as i:
                    for q in range(0, RING, 2):
                        dve.wait_ge(ev_ready, L * EV_LAYER + i * 2 + (EV_RET + q // 2 + 1))
                        job_done(r + JOB_RET // RING + i, q + 1)
                        V.tensor_tensor(Alf[:, i * 2 + q // 2, :], Bf[:, q, :], ps[:, q + 1, :],
                                        ALU.mult).then_inc(bank_free, 2)

                V.memset(z[:, :, 0:2], 0.0)
                with dve.Fori(0, DT // RING) as i:
                    for t in range(RING):
                        s = 3 * t
                        rs = lambda s: r + JOB_CONV // RING + i * 3 + s // RING
                        m = i * RING + t
                        dve.wait_ge(ev_ready, L * EV_LAYER + i * RING + (EV_CONV + t + 1))
                        job_done(rs(s + 1), (s + 1) % RING)
                        V.tensor_tensor(z[:, t % 2, 2:S + 2], Cf[:, s % RING, :], ps[:, (s + 1) % RING, :],
                                        ALU.mult).then_inc(bank_free, 2)
                        fence()
                        V.tensor_scalar(Cf[:, 4, :], z[:, t % 2, 2:S + 2], column(PAR_CONV + 2 * DT, L, m), None, ALU.mult)
                        fence()
                        V.scalar_tensor_tensor(out=Cf[:, 5, :], in0=z[:, t % 2, 1:S + 1],
                                               scalar=column(PAR_CONV + DT, L, m), in1=Cf[:, 4, :],
                                               op0=ALU.mult, op1=ALU.add)
                        fence()
                        V.scalar_tensor_tensor(out=Cf[:, 4, :], in0=z[:, t % 2, 0:S],
                                               scalar=column(PAR_CONV, L, m), in1=Cf[:, 5, :],
                                               op0=ALU.mult, op1=ALU.add)
                        fence()
                        job_done(rs(s + 2), (s + 2) % RING)
                        V.tensor_tensor(Blf[:, m, :], Cf[:, 4, :], ps[:, (s + 2) % RING, :],
                                        ALU.mult).then_inc(bank_free, 1)
                        split(Blf[:, m, :], B_hi[:, m, :], B_lo[:, m, :])

                with dve.Fori(0, PAIR_JOBS // RING) as i:
                    for q in range(0, RING, 2):
                        m = i * 2 + q // 2
                        dve.wait_ge(ev_ready, L * EV_LAYER + i * 2 + (EV_MIX + q // 2 + 1))
                        job_done(r + JOB_MIX // RING + i, q + 1)
                        V.tensor_tensor(Cf[:, 4, :], Cf[:, q, :], ps[:, q + 1, :], ALU.mult).then_inc(bank_free, 2)
                        fence()
                        V.tensor_tensor(Alf[:, m, :], Cf[:, 4, :], Alf[:, m, :], ALU.add)
                        split(Alf[:, m, :], A_hi[:, m, :], A_lo[:, m, :])

                for i in range(O_JOBS // RING):
                    for q in range(RING):
                        last = add_to_stream(r + (JOB_O // RING + i), i, q, True, i == 0 and q == 0)
                last.then_inc(ss_ready, 1)
                norm(2 * L + 1, lambda m: column(PAR_NORM2 + m, L))

                def ff_up(n_ev, hi, lo, lo_f):
                    with dve.Fori(0, DT // RING) as i:
                        for q in range(RING):
                            m = i * RING + q
                            dve.wait_ge(ev_ready, n_ev + i * RING + (q + 1))
                            V.tensor_tensor(lo_f[:, m, :], E[:, q, :], ps[:, q, :], ALU.mult).then_inc(bank_free, 1)
                            split(lo_f[:, m, :], hi[:, m, :], lo[:, m, :])

                def ff_down(rg, last_group):
                    if not last_group:
                        with dve.Fori(0, DT // RING) as i:
                            for q in range(RING):
                                add_to_stream(rg + i, i, q)
                        return
                    for i in range(DT // RING):
                        for q in range(RING):
                            last = add_to_stream(rg + i, i, q, True, i == 0 and q == 0)
                    last.then_inc(ss_ready, 1)

                def mod_sums(g):
                    dve.wait_ge(mod_loaded, (L * FF_GROUPS + g + 1) * 16)
                    for who, tiles, acc in ((1, MOD_CTX, ctx_acc[:, :, :]), (0, MOD_GROUP, mod_w[:, :, 0:P])):
                        V.tensor_scalar(acc, mod_w[:, 0:tiles, 0:P], cond[:, 0, who:who + 1], None, ALU.mult)
                        for k in range(1, DT):
                            fence()
                            last = V.scalar_tensor_tensor(out=acc, in0=mod_w[:, 0:tiles, k * P:(k + 1) * P],
                                                          scalar=cond[:, k, who:who + 1], in1=acc,
                                                          op0=ALU.mult, op1=ALU.add)
                    last.then_inc(mod_summed, 1)

                for g in range(FF_GROUPS):
                    rg = r + (JOB_FF + g * FF_GROUP_JOBS) // RING
                    ff_up(L * EV_LAYER + (EV_FF + g * DT),
                          *((A_hi, A_lo, Alf) if g % 2 == 0 else (C_hi, C_lo, Clf)))
                    mod_sums(g)
                    ff_down(rg + DT // RING, g == FF_GROUPS - 1)

                dve.wait_ge(mod_used, L * FF_GROUPS + (FF_GROUPS + 1))
                lanes = L * (2 * MOD_LAYER)
                V.tensor_tensor(mod[:, bass.ds(lanes, 2 * MOD_LAYER)], ps[:, MOD_BANK, 0:2 * MOD_LAYER],
                                par[:, bass.ds(lanes + PAR_BMOD, 2 * MOD_LAYER)], ALU.add)
                lanes = L * (2 * DT)
                V.tensor_tensor(mod_ctx[:, bass.ds(lanes, 2 * DT)], ps[:, MOD_BANK, 2 * MOD_LAYER:2 * MOD_LAYER + 2 * DT],
                                par[:, bass.ds(lanes + PAR_BCTX, 2 * DT)], ALU.add)

            def by_column(ap):
                return ap.rearrange("p (r c) -> p c r", c=GRID_W)

            def in_columns(ap):
                return ap.rearrange("p (c r) -> p c r", r=GRID_H)

            for a, (which, who, gain) in enumerate(((SC1, 0, PAR_N1), (SC1, 1, PAR_N1), (SC2, 0, PAR_N2))):
                fence()
                tiles = MOD_CTX if which < 2 else MOD_REST
                V.scalar_tensor_tensor(out=gains[:, a * DT:(a + 1) * DT].rearrange("p (g s) -> p g s", s=tiles),
                                       in0=all_of(which, who), scalar=1.0,
                                       in1=par[:, gain:gain + DT].rearrange("p (g s) -> p g s", s=tiles),
                                       op0=ALU.add, op1=ALU.mult)
            V.tensor_scalar(gains[:, 3 * DT:3 * DT + 1], par[:, PAR_QG:PAR_QG + 1], -HD ** -0.5, None, ALU.mult)

            dve.wait_ge(rt_ready, 2 * DEPTH + 1)
            V.reciprocal(E[:, ROOT, :], E[:, ROOT, :])
            fence()
            for m in range(DT + 1):
                if m < DT:
                    V.scalar_tensor_tensor(out=X[:, m, :], in0=X[:, m, :],
                                           scalar=par[:, PAR_FINAL + m:PAR_FINAL + m + 1],
                                           in1=E[:, ROOT, :], op0=ALU.mult, op1=ALU.mult).then_inc(xn_ready, 1)
                if m:
                    dve.wait_ge(xn_squared, m)
                    last = add_square(m - 1)
            last.then_inc(ss_ready, 1)
            dve.wait_ge(ctx_squared, 1)
            V.tensor_reduce(ctx_sum[:, :], ctx_sq[:, :, :].rearrange("p k t -> p t k"), AX_X,
                            ALU.add).then_inc(ctx_ss_ready, 1)

            def adaptive(v, gain0, shift, columns_order):
                dve.wait_ge(rt_ready, v + 1)
                V.reciprocal(E[:, ROOT, :], E[:, ROOT, :])
                fence()
                def scaled(m):
                    src, rstd, dst = X[:, m, :], E[:, ROOT, :], Hlf[:, m, :]
                    if columns_order:
                        src, rstd, dst = by_column(src), by_column(rstd), in_columns(dst)
                    V.scalar_tensor_tensor(out=dst, in0=src, scalar=gains[:, gain0 + m:gain0 + m + 1], in1=rstd,
                                           op0=ALU.mult, op1=ALU.mult).then_inc(h_scaled, 1)

                def low(m):
                    dve.wait_ge(h_high, (v - 1) * DT + (m + 1))
                    V.scalar_tensor_tensor(out=H_lo[:, m, :], in0=Hlf[:, m, :], scalar=vector(shift, m),
                                           in1=H_hi[:, m, :].bitcast(F32), op0=ALU.add,
                                           op1=ALU.subtract).then_inc(tiles_ready, 1)

                scaled(0)
                for m in range(DT):
                    if m + 1 < DT:
                        scaled(m + 1)
                    low(m)

            adaptive(2 * DEPTH + 1, 0, SH1, True)
            dve.wait_ge(ctx_rt_ready, 1)
            V.reciprocal(ctx_root[:, :], ctx_root[:, :])
            fence()
            for m in range(DT + 1):
                if m < DT:
                    V.scalar_tensor_tensor(out=HC_lo_f[:, m, :], in0=ctx_sb[:, m, :],
                                           scalar=gains[:, DT + m:DT + m + 1], in1=ctx_root[:, :],
                                           op0=ALU.mult, op1=ALU.mult).then_inc(hc_scaled, 1)
                if m:
                    dve.wait_ge(hc_high, m)
                    V.scalar_tensor_tensor(out=HC_lo[:, m - 1, :], in0=HC_lo_f[:, m - 1, :],
                                           scalar=vector(SH1, m - 1, 1), in1=HC_hi[:, m - 1, :].bitcast(F32),
                                           op0=ALU.add, op1=ALU.subtract).then_inc(hc_ready, 1)
            V.memset(bias[:, :, :], 0.0)
            fence()
            V.memset(bias[:, :, REAL[0].stop:KEYS], MASKED)
            V.memset(bias[:, :, 2 * UNIT_KEYS:2 * UNIT_KEYS + REAL[2].start], MASKED)
            dve.drain()
            dve.sem_inc(min_ready, 2 * TOK)

            def quarter(b, half):
                r0 = b * (2 * QT_JOBS // RING) + ATT_ROUND
                item0 = b * (2 * ITEMS) + half * ITEMS
                unit0 = (b * 2 + half) * QT_UNITS
                q_gain, k_gain = gains[:, 3 * DT:3 * DT + 1], par[:, PAR_KG:PAR_KG + 1]

                def item(i):
                    s, is_ctx = ((0, False), (1, False), (2, True), (2, False), (3, True), (3, False))[i]
                    t = s % 2
                    width = CTX if is_ctx else S
                    first = t * (S + CTX) + (S if is_ctx else 0)
                    whole, hi, lo = ([a[:, t, :] for a in (q_lo_f, q_hi, q_lo)] if s < 2 else
                                     [a[:, first:first + width] for a in (k_lo_f, k_hi, k_lo)])
                    n = half * QT_JOBS + s
                    src = ps[:, 6 + t, 0:CTX] if is_ctx else ps[:, n % RING, :]
                    dve.wait_ge(hn_root, item0 + (i + 1))
                    V.reciprocal(head_root[:, i % 2, 0:width], head_root[:, i % 2, 0:width])
                    fence()
                    mul = V.scalar_tensor_tensor(out=whole, in0=src, scalar=q_gain if s < 2 else k_gain,
                                                 in1=head_root[:, i % 2, 0:width], op0=ALU.mult, op1=ALU.mult)
                    mul.then_inc(kc_read if is_ctx else bank_free, 1)
                    split(whole, hi, lo, item_ready)

                def least(u):
                    hh, i = divmod(u, TOK)
                    s, o = u % 3, KIND[i] * UNIT_KEYS
                    if i == 0:
                        dve.wait_ge(bias_ready, (b * 2 + half) * QT_HEADS + (hh + 1))
                    dve.wait_ge(s_ready, unit0 + (u + 1))
                    V.memset(stat[:, IDLE + s:IDLE + s + 1], 0.0)
                    V.tensor_tensor_reduce(prob[:, s, :], ps[:, SCORE_BANKS[s], :], bias[:, hh % 2, o:o + UNIT_KEYS],
                                           1.0, BIG, ALU.add, ALU.min, stat[:, MIN + s:MIN + s + 1]).then_inc(min_ready, 1)

                def divide(u):
                    s = u % 3
                    dve.wait_ge(exp_ready, unit0 + (u + 1))
                    V.reciprocal(stat[:, INV + s:INV + s + 1], stat[:, SUM + s:SUM + s + 1])
                    fence()
                    V.tensor_scalar(prob[:, s, :], prob[:, s, :], stat[:, INV + s:INV + s + 1], None,
                                    ALU.mult).then_inc(prob_ready, 1)

                def output(hh):
                    rows = slice(HD * (hh % 2), HD * (hh % 2) + HD)
                    m = (b * 2 + half) * QT_TILES + hh // 2
                    dve.wait_ge(o_ready, (b * 2 + half) * QT_HEADS + (hh + 1))
                    V.tensor_copy(A_hi[rows, m, :], ps[rows, 2 + hh % 2, :])
                    fence()
                    V.tensor_tensor(A_lo[rows, m, :], ps[rows, 2 + hh % 2, :], A_hi[rows, m, :].bitcast(F32),
                                    ALU.subtract).then_inc(o_split, 1)

                for i in range(ITEMS):
                    item(i)
                for t in range(QT_TILES):
                    n = half * QT_JOBS + 2 * QT_TILES + t
                    job_done(r0 + n // RING, n % RING)
                    V.tensor_copy(vt[:, t, :], ps[:, n % RING, :]).then_inc(bank_free, 1)
                    V.tensor_copy(vt_ctx[:, t, :], ps[:, 6 + t, CTX:2 * CTX]).then_inc(vt_ready, 1)
                for bank in range(4):
                    first, count = 2 * bank, 2 if bank < 3 else 1
                    dve.wait_ge(v_mm, (b * 2 + half) * 4 + (bank + 1))
                    V.tensor_copy(v_sb[:, first:first + count, :].rearrange("p a v -> p (a v)"),
                                  ps[:, 4 + bank, 0:count * V_COLS]).then_inc(v_ready, 1)

                least(0)
                least(1)
                divide(0)
                for u in range(QT_UNITS):
                    if u + 2 < QT_UNITS:
                        least(u + 2)
                    if u + 1 < QT_UNITS:
                        divide(u + 1)
                    if u % TOK == 2 and u > TOK:
                        output(u // TOK - 1)
                output(QT_HEADS - 1)

            with dve.Fori(0, QUARTERS // 2) as b:
                for half in range(2):
                    quarter(b, half)

            for i in range(DT // RING):
                for q in range(RING):
                    m = i * RING + q
                    job_done(WO_ROUND + i, q)
                    V.scalar_tensor_tensor(out=by_column(X[:, m, :]), in0=in_columns(ps[:, q, :]), scalar=vector(G1, m),
                                           in1=by_column(X[:, m, :]), op0=ALU.mult, op1=ALU.add).then_inc(bank_free, 1)
                    last = sum_squares(m, m == 0)
            last.then_inc(ss_ready, 1)
            V.memset(gated[:, :, 0:1], 0.0)
            V.memset(gated[:, :, S + 1:S + 2], 0.0)
            adaptive(2 * DEPTH + 2, 2 * DT, SH2, False)

            r, m0 = FF2_ROUND, 0
            for g, kt in enumerate(FF2_GROUPS):
                hi, lo, lo_f = ((A_hi, A_lo, Alf), (B_hi, B_lo, Blf))[g % 2]
                with dve.Fori(0, 2 * kt // RING) as i:
                    for t in range(2):
                        m = i * 2 + (m0 + t)
                        col = lambda tap: par[:, bass.ds(m + (PAR_CONV2 + tap * FF2_T), 1)]
                        fence()
                        dve.wait_ge(ev_ready, m * 2 + (ATT_EV + 1))
                        V.tensor_scalar(conv[:, t, :], gated[:, t, 1:S + 1], col(1), None, ALU.mult)
                        fence()
                        V.scalar_tensor_tensor(out=conv[:, t, :], in0=gated[:, t, 0:S], scalar=col(0), in1=conv[:, t, :],
                                               op0=ALU.mult, op1=ALU.add)
                        fence()
                        V.scalar_tensor_tensor(out=conv[:, t, :], in0=gated[:, t, 2:S + 2], scalar=col(2),
                                               in1=conv[:, t, :], op0=ALU.mult, op1=ALU.add).then_inc(conv_ready, 1)
                        dve.wait_ge(ev_ready, m * 2 + (ATT_EV + 2))
                        job_done(r + i, 2 * t + 1)
                        k = i * 2 + t
                        V.tensor_tensor(lo_f[:, k, :], conv[:, t, :], ps[:, 2 * t + 1, :], ALU.mult).then_inc(bank_free, 2)
                        split(lo_f[:, k, :], hi[:, k, :], lo[:, k, :])
                r += 2 * kt // RING
                m0 += kt
                for i in range(DT // RING):
                    for q in range(RING):
                        m = i * RING + q
                        job_done(r + i, q)
                        add = V.scalar_tensor_tensor(out=X[:, m, :], in0=ps[:, q, :], scalar=vector(G2, m),
                                                     in1=X[:, m, :], op0=ALU.mult, op1=ALU.add)
                        add.then_inc(bank_free, 1)
                r += DT // RING



def tiles_of(w):
    k, m = w.shape
    return w.reshape(k // P, P, m // P, P).transpose(2, 1, 0, 3).reshape(m // P, P, k)


def columns(v):
    return np.ascontiguousarray(v.reshape(-1, P).T)


def hybrid_stream(w_in, w_conv_out, w_ret_out, w_o, w_up, w_down):
    t = tiles_of(w_in)
    conv_b, conv_c, conv_u = t[0:DT], t[DT:2 * DT], t[2 * DT:3 * DT]
    at = 3 * DT
    qk = t[at:at + QK_JOBS]
    v = w_in[:, (at + QK_JOBS) * P:(at + QK_JOBS + V_JOBS) * P]
    v = v.reshape(-1, V_TILES, P, V_JOBS * P // V_WIDE, V_WIDE).transpose(3, 0, 2, 1, 4).reshape(-1, P, D)
    g = t[at + QK_JOBS + V_JOBS:at + QK_JOBS + V_JOBS + G_JOBS]
    gate_a, gate_b = t[-2 * DT:-DT], t[-DT:]
    both = lambda *parts: np.stack(parts, 1).reshape(-1, P, D)
    blocks = [v, qk, g, both(gate_b, tiles_of(w_ret_out)), both(conv_c, conv_u, conv_b),
              both(gate_a, tiles_of(w_conv_out)), tiles_of(w_o)]
    for i in range(FF_GROUPS):
        blocks += [tiles_of(w_up[:, i * D:(i + 1) * D]), tiles_of(w_down[i * D:(i + 1) * D])]
    return np.concatenate(blocks)


def decay_table():
    log_gamma = np.log1p(-np.exp2(-5.0 - np.arange(RH)))
    rel = np.arange(S)[None, :] - np.arange(P)[:, None]
    t = np.where(rel >= 0, np.exp(log_gamma[:, None, None] * np.maximum(rel, 0)), 0.0) * RQK ** -0.5
    return np.ascontiguousarray(t.transpose(1, 0, 2).astype(np.float32))


def stream_of_features(x):
    return np.ascontiguousarray(x.T.reshape(-1, P, x.shape[0]).transpose(1, 0, 2))


def attention_stream(w_qkv, w_o, w_up, w_down):
    q, k, v = (tiles_of(w_qkv[:, i * D:(i + 1) * D]) for i in range(3))
    up = tiles_of(w_up)
    a, g = up[:FF2_T], up[FF2_T:]
    blocks = []
    for i in range(QUARTERS):
        t = slice(i * QT_TILES, (i + 1) * QT_TILES)
        blocks += [q[t], k[t], v[t]]
    blocks.append(tiles_of(w_o))
    m = 0
    for kt in FF2_GROUPS:
        blocks.append(np.stack([g[m:m + kt], a[m:m + kt]], 1).reshape(-1, P, D))
        down = tiles_of(w_down[m * P:(m + kt) * P])
        blocks.append(np.pad(down, ((0, 0), (0, 0), (0, D - down.shape[2]))))
        m += kt
    return np.concatenate(blocks)


def key_masks():
    masks = []
    for tile, kind in ((0, 0), (1, 1), (3, 2)):
        qc = tile * (P // GRID_H) + np.arange(P) // GRID_H
        kc = (KEY0[tile] + np.arange(KEYS)) // GRID_H
        first = np.clip(qc - WIN // 2, 0, GRID_W - WIN)[:, None]
        masks.append(np.where((kc >= first) & (kc < first + WIN), 0.0, MASKED)[:, REAL[kind]])
    return np.concatenate(masks, 1).astype(np.float32)


def toeplitz_biases(rpb):
    reach_left = WIN // 2
    cq, rq = np.arange(P) // GRID_H, np.arange(P) % GRID_H
    cl, rk = np.arange(REACH) // GRID_H - reach_left, np.arange(REACH) % GRID_H
    wide = np.pad(rpb, ((0, 2), (0, 0), (P // GRID_H, P // GRID_H + REACH_COLS)))
    dr = rk[None, :] - rq[:, None] + GRID_H - 1
    dc = cl[None, :] - cq[:, None] + WIN - 1 + P // GRID_H
    return np.ascontiguousarray(wide[:, dr, dc])


def parameters(a):
    layers = [np.concatenate([columns(a["norm_mix"][l]), columns(a["norm_mlp"][l]), columns(a["ret_norm"][l]),
                              columns(a["conv_w"][l].reshape(-1))], 1) for l in range(DEPTH)]
    half = RQK // 2
    freq = (np.float32(ROPE_BASE) ** (-np.arange(half, dtype=np.float32) / np.float32(half))).astype(np.float32)
    cond = np.stack([columns(a["c_2"][0]), columns(a["c_ctx_2"])], 2).reshape(P, -1)
    parts = layers + [
        columns(a["norm_final"]), columns(a["l0_norm1_2"]), columns(a["l0_norm2_2"]),
        np.tile(a["l0_na_q_gain_2"], 2)[:, None], np.tile(a["l0_na_k_gain_2"], 2)[:, None],
        columns(a["l0_ffn_conv_w_2"].reshape(-1)), columns(a["l0_ffn_conv_b_2"]),
        np.repeat(columns(a["l0_b_mod_2"])[:, MOD_ORDER], 2, axis=1),
        np.repeat(columns(a["l0_b_mod_2"])[:, :2 * DT], 2, axis=1), np.tile(freq, 2)[:, None], cond]
    p = np.concatenate(parts, 1)
    return np.pad(p, ((0, 0), (0, PARAMS - p.shape[1])))


def kernel(**inputs):
    import concourse.bacc as bacc
    from concourse.bass_utils import run_bass_kernel_spmd

    a = {k: np.asarray(v) for k, v in inputs.items()}
    blocks = [hybrid_stream(*(a[n][l] for n in ("w_in", "w_conv_out", "w_ret_out", "w_o", "w_up", "w_down")))
              for l in range(DEPTH)]
    blocks.append(attention_stream(a["l0_na_w_qkv_2"], a["l0_na_w_o_2"], a["l0_ffn_w_up_2"], a["l0_ffn_w_down_2"]))
    mod_blocks = tiles_of(a["l0_w_mod_2"])[MOD_ORDER].reshape(-1, MOD_GROUP, P, D).transpose(0, 2, 1, 3)
    head_rows = np.arange(P) // HD
    arrays = {
        "x": stream_of_features(a["x"][0]),
        "context": stream_of_features(a["ctx_2"][0]),
        "weights": np.concatenate(blocks),
        "mod_weights": np.ascontiguousarray(mod_blocks),
        "params": parameters(a),
        "positions": np.ascontiguousarray(np.broadcast_to(a["positions"], (P, S))),
        "decay": decay_table(),
        "key_mask": key_masks(),
        "biases": toeplitz_biases(a["l0_na_rpb_2"]),
        "block_ones": (head_rows[:, None] == head_rows[None, :]).astype(np.float32),
        "identity": np.eye(P, dtype=np.float32),
    }
    nc = bacc.Bacc("TRN2", target_bir_lowering=False, num_devices=1)
    args = [nc.dram_tensor(name, v.shape, mybir.dt.from_np(v.dtype), kind="ExternalInput").ap()
            for name, v in arrays.items()]
    out = nc.dram_tensor("out", (P, DT, S), F32, kind="ExternalOutput").ap()
    build(nc, *args, out)
    got = run_bass_kernel_spmd(nc, [arrays], core_ids=[0]).results[0]["out"]
    return np.ascontiguousarray(got.transpose(2, 1, 0).reshape(1, S, D))
```
